# Optimizing a Trainium2 kernel written in Bass

```python
import jax
import jax.numpy as jnp
from jax import lax
import numpy as np

D_MODEL = 1024
BATCH = 1
SEQ = 256
DEPTH = 2

GRID_W = 64
CTX_LEN = 256
EPS = 1e-6
N_MOD = 6

ATTN_HEADS = 8
ATTN_KV_HEADS = 2
HEAD_DIM = 64
AXIS_DIM = HEAD_DIM // 2
ROPE_THETA = 10000.0
Q_BLOCK = 128

SSM_HEADS = 8
SSM_HEAD_DIM = 64
SSM_D_INNER = SSM_HEADS * SSM_HEAD_DIM
SSM_GROUPS = 2
SSM_STATE = 64
SSM_CONV_W = 3
SSM_CHUNK = 128
SSM_CONV_DIM = SSM_D_INNER + 2 * SSM_GROUPS * SSM_STATE

Q_DIM = ATTN_HEADS * HEAD_DIM
KV_DIM = ATTN_KV_HEADS * HEAD_DIM
IDX_K = Q_DIM
IDX_V = IDX_K + KV_DIM
IDX_Z = IDX_V + KV_DIM
IDX_XBC = IDX_Z + SSM_D_INNER
IDX_DT = IDX_XBC + SSM_CONV_DIM
IN_PROJ_DIM = IDX_DT + 2 * SSM_HEADS
MIX_OUT_DIM = Q_DIM + SSM_D_INNER

SC_CONV_W = 3

FFN_HIDDEN = -(-(8 * D_MODEL) // (3 * 256)) * 256

N_EVEN = (DEPTH + 1) // 2
N_ODD = DEPTH // 2


def rms_norm(x, g):
    xf = x.astype(jnp.float32)
    y = xf * lax.rsqrt(jnp.mean(xf * xf, axis=-1, keepdims=True) + EPS)
    return (y * g.astype(jnp.float32)).astype(x.dtype)

def modulate(h, shift, scale):
    return h * (1 + scale) + shift

def swiglu(h, w_gate, w_up, w_down):
    return (jax.nn.silu(h @ w_gate) * (h @ w_up)) @ w_down

def dw_conv(x, w, b=None):
    y = lax.conv_general_dilated(
        x, w[:, None, :].astype(x.dtype), window_strides=(1,), padding='SAME',
        dimension_numbers=('NWC', 'WIO', 'NWC'), feature_group_count=x.shape[-1])
    if b is not None:
        y = y + b
    return y

def axial_rope_tables(n_tokens):
    rows = n_tokens // GRID_W
    row = jnp.repeat(jnp.arange(rows), GRID_W).astype(jnp.float32)
    col = jnp.tile(jnp.arange(GRID_W), rows).astype(jnp.float32)
    inv = 1.0 / (ROPE_THETA ** (jnp.arange(0, AXIS_DIM, 2, dtype=jnp.float32) / AXIS_DIM))
    ang = jnp.concatenate([row[:, None] * inv, col[:, None] * inv], axis=-1)
    return jnp.cos(ang), jnp.sin(ang)

def apply_rope(x, cos, sin):
    xf = x.astype(jnp.float32).reshape(x.shape[:-1] + (HEAD_DIM // 2, 2))
    x0, x1 = xf[..., 0], xf[..., 1]
    cs, sn = cos[None, :, None, :], sin[None, :, None, :]
    out = jnp.stack([x0 * cs - x1 * sn, x0 * sn + x1 * cs], axis=-1)
    return out.reshape(x.shape).astype(x.dtype)

def attn_heads(p, q_norm, k_norm):
    b, t = p.shape[:2]
    q = rms_norm(p[..., :IDX_K].reshape(b, t, ATTN_HEADS, HEAD_DIM), q_norm)
    k = rms_norm(p[..., IDX_K:IDX_V].reshape(b, t, ATTN_KV_HEADS, HEAD_DIM), k_norm)
    v = p[..., IDX_V:IDX_Z].reshape(b, t, ATTN_KV_HEADS, HEAD_DIM)
    return q, k, v

def attend_blocks(q, keys, vals):
    b, t = q.shape[:2]
    grp = ATTN_HEADS // ATTN_KV_HEADS
    nb = t // Q_BLOCK
    qb = q.reshape(b, nb, Q_BLOCK, ATTN_KV_HEADS, grp, HEAD_DIM).transpose(1, 0, 2, 3, 4, 5)
    scale = HEAD_DIM ** -0.5

    def block(qi):
        s = jnp.einsum('bqkgd,bskd->bkgqs', qi, keys).astype(jnp.float32) * scale
        pr = jax.nn.softmax(s, axis=-1).astype(vals.dtype)
        return jnp.einsum('bkgqs,bskd->bqkgd', pr, vals)

    o = lax.map(block, qb)
    return o.transpose(1, 0, 2, 3, 4, 5).reshape(b, t, Q_DIM)

def segsum_exp(a):
    l = a.shape[-1]
    mask = jnp.tril(jnp.ones((l, l), dtype=bool))
    return jnp.exp(jnp.where(mask, a[..., :, None] - a[..., None, :], -jnp.inf))

def ssd_scan(xs, dt, a, bm, cm, h0):
    b, t, nh, p = xs.shape
    g, n = bm.shape[2], bm.shape[3]
    e = nh // g
    nc, l = t // SSM_CHUNK, SSM_CHUNK
    f32 = jnp.float32
    x = xs.astype(f32).reshape(b, nc, l, g, e, p)
    dtc = dt.astype(f32).reshape(b, nc, l, g, e)
    bc = bm.astype(f32).reshape(b, nc, l, g, n)
    cc = cm.astype(f32).reshape(b, nc, l, g, n)
    a_cs = jnp.cumsum(dtc * a.astype(f32).reshape(g, e), axis=2).transpose(0, 3, 4, 1, 2)
    xdt = x * dtc[..., None]
    cb = jnp.einsum('bclgn,bcsgn->bcgls', cc, bc)
    y_diag = jnp.einsum('bcgls,bgecls,bcsgep->bclgep', cb, segsum_exp(a_cs), xdt)
    decay_to_end = jnp.exp(a_cs[..., -1:] - a_cs)
    states = jnp.einsum('bclgn,bgecl,bclgep->bcgepn', bc, decay_to_end, xdt)
    chunk_decay = jnp.exp(a_cs[..., -1]).transpose(3, 0, 1, 2)

    def step(h, inp):
        dcy, st = inp
        return h * dcy[..., None, None] + st, h

    h_init = h0.astype(f32).reshape(b, g, e, p, n)
    h_final, h_in = lax.scan(step, h_init, (chunk_decay, states.transpose(1, 0, 2, 3, 4, 5)))
    y_off = jnp.einsum('bclgn,bgecl,cbgepn->bclgep', cc, jnp.exp(a_cs), h_in)
    y = (y_diag + y_off).reshape(b, t, nh, p)
    return y.astype(xs.dtype), h_final.reshape(b, nh, p, n)

def ssd_mixer(p, conv_w, conv_b, dt_bias, a_log, d_skip, ssm_norm, h0_f, h0_b):
    b, t = p.shape[:2]
    z = p[..., IDX_Z:IDX_XBC]
    xbc = jax.nn.silu(dw_conv(p[..., IDX_XBC:IDX_DT], conv_w, conv_b))
    xs = xbc[..., :SSM_D_INNER].reshape(b, t, SSM_HEADS, SSM_HEAD_DIM)
    bm = xbc[..., SSM_D_INNER:SSM_D_INNER + SSM_GROUPS * SSM_STATE].reshape(b, t, SSM_GROUPS, SSM_STATE)
    cm = xbc[..., SSM_D_INNER + SSM_GROUPS * SSM_STATE:].reshape(b, t, SSM_GROUPS, SSM_STATE)
    dt = jax.nn.softplus(p[..., IDX_DT:].astype(jnp.float32).reshape(b, t, 2, SSM_HEADS)
                         + dt_bias.astype(jnp.float32))
    a = -jnp.exp(a_log.astype(jnp.float32))
    y_f, h_f = ssd_scan(xs, dt[:, :, 0], a[0], bm, cm, h0_f)
    flip = lambda u: jnp.flip(u, axis=1)
    y_b, h_b = ssd_scan(flip(xs), flip(dt[:, :, 1]), a[1], flip(bm), flip(cm), h0_b)
    y = (y_f + flip(y_b) + xs * d_skip[:, None]).reshape(b, t, SSM_D_INNER)
    gy = (y.astype(jnp.float32) * jax.nn.silu(z.astype(jnp.float32))).reshape(b, t, SSM_GROUPS, -1)
    gy = gy * lax.rsqrt(jnp.mean(gy * gy, axis=-1, keepdims=True) + EPS)
    out = gy.reshape(b, t, SSM_D_INNER) * ssm_norm.astype(jnp.float32)
    return out.astype(p.dtype), h_f, h_b

def hybrid_mixer(h_lat, h_ctx, w_in, q_norm, k_norm, conv_w, conv_b, dt_bias, a_log, d_skip,
                 ssm_norm, w_out, cos, sin, ctx_out):
    p_lat = h_lat @ w_in
    p_ctx = h_ctx @ w_in
    qc, kc, vc = attn_heads(p_ctx, q_norm, k_norm)
    q, k, v = attn_heads(p_lat, q_norm, k_norm)
    q, k = apply_rope(q, cos, sin), apply_rope(k, cos, sin)
    a_lat = attend_blocks(q, jnp.concatenate([k, kc], axis=1), jnp.concatenate([v, vc], axis=1))
    b = h_lat.shape[0]
    zeros = jnp.zeros((b, SSM_HEADS, SSM_HEAD_DIM, SSM_STATE), jnp.float32)
    y_ctx, hf_ctx, hb_ctx = ssd_mixer(p_ctx, conv_w, conv_b, dt_bias, a_log, d_skip, ssm_norm, zeros, zeros)
    y_lat, _, _ = ssd_mixer(p_lat, conv_w, conv_b, dt_bias, a_log, d_skip, ssm_norm, hf_ctx, hb_ctx)
    m_lat = jnp.concatenate([a_lat, y_lat], axis=-1) @ w_out
    m_ctx = None
    if ctx_out:
        a_ctx = attend_blocks(qc, kc, vc)
        m_ctx = jnp.concatenate([a_ctx, y_ctx], axis=-1) @ w_out
    return m_lat, m_ctx

def shortconv_mixer(h, w_in, conv_w, w_out):
    gb, gc, u = jnp.split(h @ w_in, 3, axis=-1)
    return (gb * dw_conv(gc * u, conv_w)) @ w_out

def first_inputs(seed: int = 0) -> dict:
    key = jax.random.key(seed)
    ks = iter(jax.random.split(key, 40))
    f32 = jnp.float32
    d = D_MODEL

    def nrm(shape, fan_in):
        return jax.random.normal(next(ks), shape, f32) * (fan_in ** -0.5)

    def gain(shape):
        return 1.0 + 0.05 * jax.random.normal(next(ks), shape, f32)

    x = jax.random.normal(next(ks), (BATCH, SEQ, d), f32)
    c = jax.random.normal(next(ks), (BATCH, d), f32)
    ctx = jax.random.normal(next(ks), (BATCH, CTX_LEN, d), f32)
    c_ctx = jax.random.normal(next(ks), (d,), f32)
    ada_w = 0.5 * nrm((DEPTH, d, N_MOD * d), d)
    ada_b = 0.02 * jax.random.normal(next(ks), (DEPTH, N_MOD * d), f32)
    norm_mix = gain((DEPTH, d))
    norm_ffn = gain((DEPTH, d))
    ffn_w_gate = nrm((DEPTH, d, FFN_HIDDEN), d)
    ffn_w_up = nrm((DEPTH, d, FFN_HIDDEN), d)
    ffn_w_down = nrm((DEPTH, FFN_HIDDEN, d), FFN_HIDDEN)
    hy_w_in = nrm((N_EVEN, d, IN_PROJ_DIM), d)
    hy_q_norm = gain((N_EVEN, HEAD_DIM))
    hy_k_norm = gain((N_EVEN, HEAD_DIM))
    hy_conv_w = nrm((N_EVEN, SSM_CONV_W, SSM_CONV_DIM), SSM_CONV_W)
    hy_conv_b = 0.02 * jax.random.normal(next(ks), (N_EVEN, SSM_CONV_DIM), f32)
    dt0 = jnp.exp(jax.random.uniform(next(ks), (N_EVEN, 2, SSM_HEADS), f32,
                                     np.log(1e-3).astype(np.float32), np.log(1e-1).astype(np.float32)))
    hy_dt_bias = dt0 + jnp.log(-jnp.expm1(-dt0))
    hy_a_log = jnp.log(jax.random.uniform(next(ks), (N_EVEN, 2, SSM_HEADS), f32, 1.0, 16.0))
    hy_d_skip = gain((N_EVEN, SSM_HEADS))
    hy_ssm_norm = gain((N_EVEN, SSM_D_INNER))
    hy_w_out = nrm((N_EVEN, MIX_OUT_DIM, d), MIX_OUT_DIM)
    sc_w_in = nrm((N_ODD, d, 3 * d), d)
    sc_conv_w = nrm((N_ODD, SC_CONV_W, d), SC_CONV_W)
    sc_w_out = nrm((N_ODD, d, d), d)
    final_norm = gain((d,))
    return {
        'x': x, 'c': c, 'ctx': ctx, 'c_ctx': c_ctx,
        'ada_w': ada_w, 'ada_b': ada_b, 'norm_mix': norm_mix, 'norm_ffn': norm_ffn,
        'ffn_w_gate': ffn_w_gate, 'ffn_w_up': ffn_w_up, 'ffn_w_down': ffn_w_down,
        'hy_w_in': hy_w_in, 'hy_q_norm': hy_q_norm, 'hy_k_norm': hy_k_norm,
        'hy_conv_w': hy_conv_w, 'hy_conv_b': hy_conv_b, 'hy_dt_bias': hy_dt_bias,
        'hy_a_log': hy_a_log, 'hy_d_skip': hy_d_skip, 'hy_ssm_norm': hy_ssm_norm, 'hy_w_out': hy_w_out,
        'sc_w_in': sc_w_in, 'sc_conv_w': sc_conv_w, 'sc_w_out': sc_w_out,
        'final_norm': final_norm,
    }

def first_block(x, c, ctx, c_ctx, ada_w, ada_b, norm_mix, norm_ffn, ffn_w_gate, ffn_w_up, ffn_w_down,
              hy_w_in, hy_q_norm, hy_k_norm, hy_conv_w, hy_conv_b, hy_dt_bias, hy_a_log, hy_d_skip,
              hy_ssm_norm, hy_w_out, sc_w_in, sc_conv_w, sc_w_out, final_norm):
    cos, sin = axial_rope_tables(x.shape[1])
    h_ctx = ctx
    for i in range(DEPTH):
        ctx_read_later = any(j % 2 == 0 for j in range(i + 1, DEPTH))
        mod = (jax.nn.silu(c) @ ada_w[i] + ada_b[i])[:, None, :]
        sh1, sc1, g1, sh2, sc2, g2 = jnp.split(mod, N_MOD, axis=-1)
        hx = modulate(rms_norm(x, norm_mix[i]), sh1, sc1)
        need_ctx_in = (i % 2 == 0) or ctx_read_later
        if need_ctx_in:
            mod_c = (jax.nn.silu(c_ctx) @ ada_w[i] + ada_b[i])[None, None, :]
            csh1, csc1, cg1, csh2, csc2, cg2 = jnp.split(mod_c, N_MOD, axis=-1)
            hc = modulate(rms_norm(h_ctx, norm_mix[i]), csh1, csc1)
        if i % 2 == 0:
            e = i // 2
            m_lat, m_ctx = hybrid_mixer(hx, hc, hy_w_in[e], hy_q_norm[e], hy_k_norm[e], hy_conv_w[e],
                                        hy_conv_b[e], hy_dt_bias[e], hy_a_log[e], hy_d_skip[e],
                                        hy_ssm_norm[e], hy_w_out[e], cos, sin, ctx_read_later)
        else:
            o = i // 2
            m_lat = shortconv_mixer(hx, sc_w_in[o], sc_conv_w[o], sc_w_out[o])
            m_ctx = shortconv_mixer(hc, sc_w_in[o], sc_conv_w[o], sc_w_out[o]) if ctx_read_later else None
        x = x + g1 * m_lat
        x = x + g2 * swiglu(modulate(rms_norm(x, norm_ffn[i]), sh2, sc2),
                            ffn_w_gate[i], ffn_w_up[i], ffn_w_down[i])
        if ctx_read_later:
            h_ctx = h_ctx + cg1 * m_ctx
            h_ctx = h_ctx + cg2 * swiglu(modulate(rms_norm(h_ctx, norm_ffn[i]), csh2, csc2),
                                         ffn_w_gate[i], ffn_w_up[i], ffn_w_down[i])
    return rms_norm(x, final_norm)


DEPTH_2 = 1

HG_HEADS = 4
HG_HEAD_DIM = 128
HG_WIDTH = HG_HEADS * HG_HEAD_DIM
DN_HEADS = 4
DN_HEAD_DIM = 128
DN_WIDTH = DN_HEADS * DN_HEAD_DIM
MIX_WIDTH = HG_WIDTH + DN_WIDTH
HG_CHUNK = 32
DN_CHUNK = 64
CONV_SIZE = 3
N_GROUPS = 4
EXPERTS_PER_GROUP = 4
N_EXPERTS = N_GROUPS * EXPERTS_PER_GROUP
TOP_K_IN_GROUP = 2
EXPERT_FF = 512
NORM_EPS = 1e-6
IN_SPLITS = [HG_WIDTH] * 5 + [DN_WIDTH] * 4 + [DN_HEADS] * 4
IN_COLS = sum(IN_SPLITS)


def rms_norm_2(x, w):
    x32 = x.astype(jnp.float32)
    y = x32 * lax.rsqrt(jnp.mean(x32 * x32, axis=-1, keepdims=True) + NORM_EPS)
    return (y * w.astype(jnp.float32)).astype(x.dtype)

def modulate_2(h, shift, scale):
    return h * (1 + scale) + shift

def l2_normalize(t):
    t32 = t.astype(jnp.float32)
    return (t32 * lax.rsqrt(jnp.sum(t32 * t32, axis=-1, keepdims=True) + NORM_EPS)).astype(t.dtype)

def to_heads(t, n_heads):
    b, length, width = t.shape
    return t.reshape(b, length, n_heads, width // n_heads).transpose(0, 2, 1, 3)

def gated_head_norm(o, gate, w):
    y = rms_norm_2(o, w) * jax.nn.silu(gate)
    b, h, length, d = y.shape
    return y.transpose(0, 2, 1, 3).reshape(b, length, h * d)

def split_in_proj(p):
    bounds = [int(v) for v in np.cumsum(IN_SPLITS)[:-1]]
    return jnp.split(p, bounds, axis=-1)

def gla_chunk_scan(q, k, v, log_f, s0):
    b, h, length, dk = q.shape
    dv = v.shape[-1]
    n = length // HG_CHUNK
    incl = jnp.tril(jnp.ones((HG_CHUNK, HG_CHUNK), dtype=bool))[:, :, None]

    def to_chunks(t):
        return jnp.moveaxis(t.reshape(b, h, n, HG_CHUNK, t.shape[-1]), 2, 0)

    def step(state, inp):
        qc, kc, vc, fc = inp
        cum = jnp.cumsum(fc, axis=2)
        diff = cum[:, :, :, None, :] - cum[:, :, None, :, :]
        decay = jnp.where(incl, jnp.exp(jnp.where(incl, diff, 0.0)), 0.0)
        attn = jnp.einsum('bhtd,bhsd,bhtsd->bhts', qc, kc, decay)
        o = jnp.einsum('bhtd,bhde->bhte', qc * jnp.exp(cum), state) + jnp.einsum('bhts,bhse->bhte', attn, vc)
        last = cum[:, :, -1, :]
        k_dec = kc * jnp.exp(last[:, :, None, :] - cum)
        state = jnp.exp(last)[..., None] * state + jnp.einsum('bhsd,bhse->bhde', k_dec, vc)
        return state, o

    state, o = lax.scan(step, s0, (to_chunks(q), to_chunks(k), to_chunks(v), to_chunks(log_f)))
    return jnp.moveaxis(o, 0, 2).reshape(b, h, length, dv), state

def gated_delta_chunk_scan(q, k, v, beta, log_a, s0):
    b, h, length, dk = q.shape
    dv = v.shape[-1]
    n = length // DN_CHUNK
    dt = q.dtype
    qn = q.reshape(b, h, n, DN_CHUNK, dk)
    kn = k.reshape(b, h, n, DN_CHUNK, dk)
    vn = v.reshape(b, h, n, DN_CHUNK, dv)
    bn = beta.reshape(b, h, n, DN_CHUNK).astype(jnp.float32)
    cum = jnp.cumsum(log_a.astype(jnp.float32).reshape(b, h, n, DN_CHUNK), axis=-1)
    incl = jnp.tril(jnp.ones((DN_CHUNK, DN_CHUNK), dtype=bool))
    strict = jnp.tril(jnp.ones((DN_CHUNK, DN_CHUNK), dtype=bool), -1)
    diff = cum[..., :, None] - cum[..., None, :]
    decay = jnp.where(incl, jnp.exp(jnp.where(incl, diff, 0.0)), 0.0)
    kk = jnp.einsum('bhntd,bhnsd->bhnts', kn, kn).astype(jnp.float32)
    a_mat = jnp.where(strict, bn[..., :, None] * kk * decay, 0.0) + jnp.eye(DN_CHUNK, dtype=jnp.float32)
    rhs = jnp.concatenate([kn.astype(jnp.float32) * (bn * jnp.exp(cum))[..., None],
                           vn.astype(jnp.float32) * bn[..., None]], axis=-1)
    sol = lax.linalg.triangular_solve(a_mat, rhs, left_side=True, lower=True, unit_diagonal=True)
    w = sol[..., :dk].astype(dt)
    u = sol[..., dk:].astype(dt)
    qk = jnp.einsum('bhntd,bhnsd->bhnts', qn, kn) * decay.astype(dt)
    q_dec = qn * jnp.exp(cum)[..., None].astype(dt)
    k_dec = kn * jnp.exp(cum[..., -1:] - cum)[..., None].astype(dt)
    g_tot = jnp.exp(cum[..., -1]).astype(dt)

    def step(state, inp):
        w_c, u_c, qk_c, qd_c, kd_c, gt_c = inp
        v_new = u_c - jnp.einsum('bhtd,bhde->bhte', w_c, state)
        o = jnp.einsum('bhtd,bhde->bhte', qd_c, state) + jnp.einsum('bhts,bhse->bhte', qk_c, v_new)
        state = gt_c[..., None, None] * state + jnp.einsum('bhtd,bhte->bhde', kd_c, v_new)
        return state, o

    xs = tuple(jnp.moveaxis(t, 2, 0) for t in (w, u, qk, q_dec, k_dec, g_tot))
    state, o = lax.scan(step, s0, xs)
    return jnp.moveaxis(o, 0, 2).reshape(b, h, length, dv), state

def run_bidirectional(scan_fn, ctx_fwd, lat_fwd, ctx_bwd, lat_bwd, s0):
    oc_f, sc_f = scan_fn(*ctx_fwd, s0)
    ox_f, _ = scan_fn(*lat_fwd, sc_f)
    oc_b, sc_b = scan_fn(*[jnp.flip(t, axis=2) for t in ctx_bwd], s0)
    ox_b, _ = scan_fn(*[jnp.flip(t, axis=2) for t in lat_bwd], sc_b)
    return oc_f + jnp.flip(oc_b, axis=2), ox_f + jnp.flip(ox_b, axis=2)

def hgrn2_log_forget(f_logit, lb):
    return jnp.logaddexp(jnp.log(lb), jnp.log1p(-lb) + jax.nn.log_sigmoid(f_logit))

def hgrn2_branch(cols_c, cols_x, lb, norm_w):
    def prep(cols):
        q, i, g, f_fwd, f_bwd = cols
        q = to_heads(jax.nn.silu(q), HG_HEADS)
        v = to_heads(i, HG_HEADS)
        per_dir = []
        for f_logit, lb_d in ((f_fwd, lb[0]), (f_bwd, lb[1])):
            log_f = to_heads(hgrn2_log_forget(f_logit, lb_d), HG_HEADS)
            per_dir.append((q, -jnp.expm1(log_f), v, log_f))
        return per_dir, to_heads(g, HG_HEADS)

    dirs_c, gc = prep(cols_c)
    dirs_x, gx = prep(cols_x)
    s0 = jnp.zeros((gc.shape[0], HG_HEADS, HG_HEAD_DIM, HG_HEAD_DIM), gc.dtype)
    oc, ox = run_bidirectional(gla_chunk_scan, dirs_c[0], dirs_x[0], dirs_c[1], dirs_x[1], s0)
    return gated_head_norm(oc, gc, norm_w), gated_head_norm(ox, gx, norm_w)

def short_conv_latent(t, w):
    b, length, ch = t.shape
    rows = length // GRID_W
    y = lax.conv_general_dilated(t.reshape(b, rows, GRID_W, ch), w[:, :, None, :], window_strides=(1, 1),
                                 padding='SAME', dimension_numbers=('NHWC', 'HWIO', 'NHWC'),
                                 feature_group_count=ch)
    return y.reshape(b, length, ch)

def short_conv_context(t, w):
    ch = t.shape[-1]
    return lax.conv_general_dilated(t, w[CONV_SIZE // 2][:, None, :], window_strides=(1,), padding='SAME',
                                    dimension_numbers=('NWC', 'WIO', 'NWC'), feature_group_count=ch)

def deltanet_branch(cols_c, cols_x, conv_w, a_log, dt_bias, norm_w):
    def prep(cols, conv_fn):
        q, k, v, z, b_fwd, b_bwd, a_fwd, a_bwd = cols
        qkv = jax.nn.silu(conv_fn(jnp.concatenate([q, k, v], axis=-1), conv_w))
        q, k, v = jnp.split(qkv, 3, axis=-1)
        q = l2_normalize(to_heads(q, DN_HEADS)) * (DN_HEAD_DIM ** -0.5)
        k = l2_normalize(to_heads(k, DN_HEADS))
        v = to_heads(v, DN_HEADS)
        per_dir = []
        for d, (b_logit, a_logit) in enumerate(((b_fwd, a_fwd), (b_bwd, a_bwd))):
            beta = jax.nn.sigmoid(b_logit).transpose(0, 2, 1)
            log_a = (-jnp.exp(a_log[d]) * jax.nn.softplus(a_logit + dt_bias[d])).transpose(0, 2, 1)
            per_dir.append((q, k, v, beta, log_a))
        return per_dir, to_heads(z, DN_HEADS)

    dirs_c, zc = prep(cols_c, short_conv_context)
    dirs_x, zx = prep(cols_x, short_conv_latent)
    s0 = jnp.zeros((zc.shape[0], DN_HEADS, DN_HEAD_DIM, DN_HEAD_DIM), zc.dtype)
    oc, ox = run_bidirectional(gated_delta_chunk_scan, dirs_c[0], dirs_x[0], dirs_c[1], dirs_x[1], s0)
    return gated_head_norm(oc, zc, norm_w), gated_head_norm(ox, zx, norm_w)

def hybrid_mixer_2(pc, px, lb, hg_norm_w, conv_w, a_log, dt_bias, dn_norm_w):
    cols_c = split_in_proj(pc)
    cols_x = split_in_proj(px)
    hg_c, hg_x = hgrn2_branch(cols_c[:5], cols_x[:5], lb, hg_norm_w)
    dn_c, dn_x = deltanet_branch(cols_c[5:], cols_x[5:], conv_w, a_log, dt_bias, dn_norm_w)
    return jnp.concatenate([hg_c, dn_c], axis=-1), jnp.concatenate([hg_x, dn_x], axis=-1)

def hierarchical_moe(h, w_group, b_group, w_expert, b_expert, w_gate, w_up, w_down):
    t = h.reshape(-1, h.shape[-1])
    g_logits = (t @ w_group + b_group).astype(jnp.float32)
    g_prob = jax.nn.softmax(g_logits, axis=-1)
    g_idx = jnp.argmax(g_logits, axis=-1)
    g_w = jnp.take_along_axis(g_prob, g_idx[:, None], axis=-1)
    e_logits = (t @ w_expert + b_expert).astype(jnp.float32).reshape(-1, N_GROUPS, EXPERTS_PER_GROUP)
    e_in_group = jnp.take_along_axis(e_logits, g_idx[:, None, None], axis=1)[:, 0]
    top_v, top_i = lax.top_k(e_in_group, TOP_K_IN_GROUP)
    top_w = jax.nn.softmax(top_v, axis=-1) * g_w
    expert_id = g_idx[:, None] * EXPERTS_PER_GROUP + top_i
    gates = jnp.sum(jax.nn.one_hot(expert_id, N_EXPERTS, dtype=jnp.float32) * top_w[..., None],
                    axis=1).astype(t.dtype)
    y = jnp.zeros_like(t)
    for e in range(N_EXPERTS):
        a = jax.nn.silu(t @ w_gate[e]) * (t @ w_up[e])
        y = y + gates[:, e:e + 1] * (a @ w_down[e])
    return y.reshape(h.shape)

def second_inputs(seed: int = 0) -> dict:
    key = jax.random.key(seed)
    ks = jax.random.split(key, 24)
    f32 = jnp.float32

    def nrm(k, shape, scale):
        return jax.random.normal(k, shape, f32) * scale

    a_init = jax.random.uniform(ks[13], (DEPTH_2, 2, DN_HEADS), f32, minval=1.0, maxval=16.0)
    dt = jnp.exp(jax.random.uniform(ks[14], (DEPTH_2, 2, DN_HEADS), f32,
                                    minval=float(np.log(1e-3)), maxval=float(np.log(1e-1))))
    return {
        'x': nrm(ks[0], (BATCH, SEQ, D_MODEL), 1.0),
        'c': nrm(ks[1], (BATCH, D_MODEL), 1.0),
        'ctx': nrm(ks[2], (BATCH, CTX_LEN, D_MODEL), 1.0),
        'c_ctx': nrm(ks[3], (D_MODEL,), 1.0),
        'w_mod': nrm(ks[4], (DEPTH_2, D_MODEL, 6 * D_MODEL), 0.5 * D_MODEL ** -0.5),
        'b_mod': nrm(ks[5], (DEPTH_2, 6 * D_MODEL), 0.02),
        'norm1_w': 1.0 + nrm(ks[6], (DEPTH_2, D_MODEL), 0.02),
        'norm2_w': 1.0 + nrm(ks[7], (DEPTH_2, D_MODEL), 0.02),
        'w_in': nrm(ks[8], (DEPTH_2, D_MODEL, IN_COLS), D_MODEL ** -0.5),
        'w_out': nrm(ks[9], (DEPTH_2, MIX_WIDTH, D_MODEL), MIX_WIDTH ** -0.5),
        'hg_lb': nrm(ks[10], (DEPTH_2, 2, HG_WIDTH), 0.1),
        'hg_norm_w': 1.0 + nrm(ks[11], (DEPTH_2, HG_HEAD_DIM), 0.02),
        'dn_conv_w': nrm(ks[12], (DEPTH_2, CONV_SIZE, CONV_SIZE, 3 * DN_WIDTH), 1.0 / CONV_SIZE),
        'dn_a_log': jnp.log(a_init),
        'dn_dt_bias': dt + jnp.log(-jnp.expm1(-dt)),
        'dn_norm_w': 1.0 + nrm(ks[15], (DEPTH_2, DN_HEAD_DIM), 0.02),
        'w_group': nrm(ks[16], (DEPTH_2, D_MODEL, N_GROUPS), D_MODEL ** -0.5),
        'b_group': nrm(ks[17], (DEPTH_2, N_GROUPS), 0.01),
        'w_expert': nrm(ks[18], (DEPTH_2, D_MODEL, N_EXPERTS), D_MODEL ** -0.5),
        'b_expert': nrm(ks[19], (DEPTH_2, N_EXPERTS), 0.01),
        'w_gate': nrm(ks[20], (DEPTH_2, N_EXPERTS, D_MODEL, EXPERT_FF), D_MODEL ** -0.5),
        'w_up': nrm(ks[21], (DEPTH_2, N_EXPERTS, D_MODEL, EXPERT_FF), D_MODEL ** -0.5),
        'w_down': nrm(ks[22], (DEPTH_2, N_EXPERTS, EXPERT_FF, D_MODEL), EXPERT_FF ** -0.5),
        'final_norm_w': 1.0 + nrm(ks[23], (D_MODEL,), 0.02),
    }

def second_block(x, c, ctx, c_ctx, w_mod, b_mod, norm1_w, norm2_w, w_in, w_out, hg_lb, hg_norm_w,
              dn_conv_w, dn_a_log, dn_dt_bias, dn_norm_w, w_group, b_group, w_expert, b_expert,
              w_gate, w_up, w_down, final_norm_w):
    lb_all = jnp.cumsum(jax.nn.softmax(hg_lb.astype(jnp.float32), axis=0), axis=0)
    lb_all = (lb_all - lb_all[0]).astype(x.dtype)
    silu_c = jax.nn.silu(c)
    silu_c_ctx = jax.nn.silu(c_ctx)
    xs, cs = x, ctx
    for l in range(DEPTH_2):
        last = l == DEPTH_2 - 1
        sh1x, sc1x, g1x, sh2x, sc2x, g2x = jnp.split((silu_c @ w_mod[l] + b_mod[l])[:, None, :], 6, axis=-1)
        sh1c, sc1c, g1c, sh2c, sc2c, g2c = jnp.split((silu_c_ctx @ w_mod[l] + b_mod[l])[None, None, :], 6, axis=-1)
        hx = modulate_2(rms_norm_2(xs, norm1_w[l]), sh1x, sc1x)
        hc = modulate_2(rms_norm_2(cs, norm1_w[l]), sh1c, sc1c)
        oc, ox = hybrid_mixer_2(hc @ w_in[l], hx @ w_in[l], lb_all[l], hg_norm_w[l], dn_conv_w[l],
                              dn_a_log[l], dn_dt_bias[l], dn_norm_w[l])
        moe_args = (w_group[l], b_group[l], w_expert[l], b_expert[l], w_gate[l], w_up[l], w_down[l])
        xs = xs + g1x * (ox @ w_out[l])
        xs = xs + g2x * hierarchical_moe(modulate_2(rms_norm_2(xs, norm2_w[l]), sh2x, sc2x), *moe_args)
        if not last:
            cs = cs + g1c * (oc @ w_out[l])
            cs = cs + g2c * hierarchical_moe(modulate_2(rms_norm_2(cs, norm2_w[l]), sh2c, sc2c), *moe_args)
    return rms_norm_2(xs, final_norm_w)


def setup_inputs(seed=0):
    out = dict(first_inputs(seed))
    for name, value in second_inputs(seed + 1).items():
        if name != "x":
            out[name + "_2"] = value
    return out


def reference(
    x, c, ctx, c_ctx, ada_w, ada_b, norm_mix, norm_ffn, ffn_w_gate, ffn_w_up, ffn_w_down,
    hy_w_in, hy_q_norm, hy_k_norm, hy_conv_w, hy_conv_b, hy_dt_bias, hy_a_log, hy_d_skip,
    hy_ssm_norm, hy_w_out, sc_w_in, sc_conv_w, sc_w_out, final_norm, c_2, ctx_2, c_ctx_2,
    w_mod_2, b_mod_2, norm1_w_2, norm2_w_2, w_in_2, w_out_2, hg_lb_2, hg_norm_w_2, dn_conv_w_2,
    dn_a_log_2, dn_dt_bias_2, dn_norm_w_2, w_group_2, b_group_2, w_expert_2, b_expert_2,
    w_gate_2, w_up_2, w_down_2, final_norm_w_2,
):
    x = first_block(
        x, c, ctx, c_ctx, ada_w, ada_b, norm_mix, norm_ffn, ffn_w_gate, ffn_w_up, ffn_w_down,
        hy_w_in, hy_q_norm, hy_k_norm, hy_conv_w, hy_conv_b, hy_dt_bias, hy_a_log, hy_d_skip,
        hy_ssm_norm, hy_w_out, sc_w_in, sc_conv_w, sc_w_out, final_norm,
    )
    return second_block(
        x, c_2, ctx_2, c_ctx_2, w_mod_2, b_mod_2, norm1_w_2, norm2_w_2, w_in_2, w_out_2,
        hg_lb_2, hg_norm_w_2, dn_conv_w_2, dn_a_log_2, dn_dt_bias_2, dn_norm_w_2, w_group_2,
        b_group_2, w_expert_2, b_expert_2, w_gate_2, w_up_2, w_down_2, final_norm_w_2,
    )


_drawn_inputs = setup_inputs


def setup_inputs(seed=0):
    import zlib

    import numpy as np

    out = dict(_drawn_inputs(seed))
    spreads = {}
    factors = {'ctx': 2.712,
     'hy_q_norm': 8.0,
     'hy_k_norm': 8.0,
     'hy_conv_b': 5.29,
     'hy_d_skip': 5.712,
     'hy_ssm_norm': 3.952,
     'ctx_2': 4.111,
     'c_ctx_2': 6.227,
     'norm1_w_2': 8.0,
     'norm2_w_2': 5.552,
     'hg_norm_w_2': 8.0,
     'dn_norm_w_2': 8.0,
     'b_group_2': 8.0,
     'b_expert_2': 53.019,
     'final_norm_w_2': 7.98}
    for name, (base, spread) in spreads.items():
        noise = np.random.default_rng([zlib.crc32(name.encode()), seed]).standard_normal(out[name].shape)
        drawn = base * np.exp(spread * noise) if base else spread * noise
        out[name] = jnp.asarray(drawn.astype(out[name].dtype))
    for name, factor in factors.items():
        out[name] = (out[name] * factor).astype(out[name].dtype)
    return out
```

```python
import numpy as np

P = 128
D = 1024
KB = D // P
T = 256
TT = 2 * T
NT = TT // P
TILE = 6144
TC = TILE // KB
TB = TC // P
SLOTS = 4
FFN = 2816
EXPERTS, EFF = 16, 512
GROUP = 256
NADA = KB
NFFN = FFN // GROUP
NMOE = EXPERTS * EFF // GROUP
EPS = 1e-6
LEVELS = (1, 2, 4, 8, 16, 32, 64)

STREAM = (("ada0", NADA), ("hy", 4), ("ffn0", NFFN), ("ada1", NADA), ("sc", 6), ("ffn1", NFFN),
          ("mod2", NADA), ("in2", 6), ("out2", 2), ("moe", NMOE))
START, NTILES = {}, 0
for _name, _n in STREAM:
    START[_name] = NTILES
    NTILES += _n

COLS = (("ident", P), ("triF", P), ("triB", P), ("afterF", P), ("afterB", P), ("ones", P), ("pair", P),
        ("rot", P), ("cos", T), ("sin", T), ("spanF", 8 * P), ("spanB", 8 * P), ("maskF", 7 * P), ("maskB", 7 * P),
        ("c", 2 * KB), ("c2", 2 * KB), ("ada_b0", 48), ("ada_b1", 48), ("mod_b2", 48),
        ("norm_mix0", KB), ("norm_mix1", KB), ("norm_ffn0", KB), ("norm_ffn1", KB), ("final1", KB),
        ("norm1_2", KB), ("norm2_2", KB), ("final2", KB),
        ("qn", 1), ("kn", 1), ("eps", 1), ("conv_w", 18), ("conv_b", 6), ("dt_bias", 16), ("a_log", 16),
        ("d_skip", 4), ("ssm_norm", 4), ("w_dt", KB * 16), ("sc_conv", KB * 3),
        ("hg_norm", 1), ("dn_conv", 12 * 9), ("dn_alog", 8), ("dn_dtb", 8), ("dn_norm", 1),
        ("w_ba", KB * 16), ("w_rt", KB * 20), ("b_rt", 20), ("first4", 4))
AT, NCOLS = {}, 0
for _name, _n in COLS:
    AT[_name] = (NCOLS, _n)
    NCOLS += _n


def build(nc, stream, params, xin, ctx1, ctx2, out):
    import concourse.bass as bass
    from concourse import mybir
    F32 = mybir.dt.float32
    U32 = mybir.dt.uint32
    ACT = mybir.ActivationFunctionType
    ALU = mybir.AluOpType
    AX = mybir.AxisListType
    MUL, ADD, SUB = ALU.mult, ALU.add, ALU.subtract

    class Line:

        def __init__(self, eng, name):
            self.eng, self.sem, self.n, self.seen = eng, nc.alloc_semaphore(name), 0, {}

        def after(self, *tokens):
            for tok in tokens:
                if tok is None:
                    continue
                sem, val, key = tok
                if val > self.seen.get(key, 0):
                    self.eng.wait_ge(sem, val)
                    self.seen[key] = val
            return self.eng

        def done(self, ins):
            self.n += 1
            ins.then_inc(self.sem, 1)
            return (self.sem, self.n, id(self))

        def last(self):
            return (self.sem, self.n, id(self))

    PE, DVE, SC, GP = (Line(nc.tensor, "pe_done"), Line(nc.vector, "dve_done"), Line(nc.scalar, "act_done"),
                       Line(nc.gpsimd, "pool_done"))
    COMPUTE = (PE, DVE, SC, GP)

    def phase():
        for line in COMPUTE:
            for other in COMPUTE:
                if other.n:
                    line.after(other.last())

    def sb(name, cols):
        return nc.alloc_sbuf_tensor(name, [P, cols], F32)[:, :]

    ring = [sb(f"ring{s}", TILE) for s in range(SLOTS)]
    par = sb("par", NCOLS)
    x = sb("x", KB * T).rearrange("p (k t) -> p k t", k=KB)
    mod = sb("mod", 48 * 2).rearrange("p (j c) -> p j c", c=2)
    gain = sb("gain", 2 * KB).rearrange("p (k c) -> p k c", c=2)
    silu_c = [sb(f"silu_c{i}", 2 * KB) for i in range(2)]
    small = sb("small", 1536)
    ARENA = (nc.sbuf_bytes_remaining - 64) // 4
    arena = sb("arena", ARENA)
    psum = [nc.alloc_psum_tensor(f"bank{b}", [P, 512], F32)[:, :] for b in range(8)]

    def cst(name):
        a, n = AT[name]
        return par[:, a:a + n]

    class Carve:

        def __init__(self, buf, size):
            self.buf, self.size, self.at = buf, size, 0

        def __call__(self, cols):
            a = self.at
            self.at += cols
            assert self.at <= self.size, (self.at, self.size)
            return self.buf[:, a:self.at]

    take = Carve(arena, ARENA)
    tiny = Carve(small, 1536)

    class Bank:

        def __init__(self):
            self.free, self.n = [None] * 8, 0

        def next(self, among=range(8)):
            b = list(among)[self.n % len(among)]
            self.n += 1
            PE.after(self.free[b])
            return b

    bank = Bank()

    landed = [nc.alloc_semaphore(f"landed{s}") for s in range(SLOTS)]
    freed = nc.alloc_semaphore("tiles_freed")
    loaded = nc.alloc_semaphore("inputs_loaded")
    sync = nc.sync

    arrays = ((par, params), (x, xin))
    for dst, src in arrays:
        sync.dma_start(dst, src).then_inc(loaded, 16)
    for s in range(SLOTS):
        sync.dma_start(ring[s], stream[s, :, :]).then_inc(landed[s], 16)
    assert NTILES % SLOTS == 0
    with sync.Fori(1, NTILES // SLOTS) as r:
        for s in range(SLOTS):
            sync.wait_ge(freed, r * SLOTS + (s + 1 - SLOTS))
            sync.dma_start(ring[s], stream[r * SLOTS + s, :, :]).then_inc(landed[s], 16)

    def slot(tile):
        return ring[tile % SLOTS]

    def arrive(tile, i=None):
        val = 16 * (tile // SLOTS + 1)
        nc.tensor.wait_ge(landed[tile % SLOTS], val if i is None else val + i * 16)

    def proj(tile):
        return slot(tile).rearrange("p (k n) -> p k n", k=KB)

    def mm(out_, lhsT, rhs, start=True, stop=True, **kw):
        return nc.tensor.matmul(out_, lhsT, rhs, start=start, stop=stop, **kw)

    def product(out_, pairs):
        for n, (a, b) in enumerate(pairs):
            ins = mm(out_, a, b, start=n == 0, stop=n == len(pairs) - 1)
        return ins

    def bc(ap, n):
        return ap.unsqueeze(2).broadcast_to([ap.shape[0], ap.shape[1], n])

    def rep(ap, n):
        return ap.unsqueeze(1).broadcast_to([ap.shape[0], n, ap.shape[1]])

    IN = (loaded, 32, "in")
    for line in (PE, DVE, SC, GP):
        line.after(IN)

    ident, ones = cst("ident"), cst("ones")
    tri = (cst("triF"), cst("triB"))
    after_ = (cst("afterF"), cst("afterB"))
    eps = cst("eps")

    t_silu = [SC.done(SC.eng.activation(silu_c[i], cst(n), ACT.Silu)) for i, n in enumerate(("c", "c2"))]
    zero = tiny(128)
    t_zero = GP.done(GP.eng.memset(zero, 0.0))

    def modulation(name, cond, bias, cols):
        b = bank.next()
        acc = psum[b][:, 0:48 * 2].rearrange("p (j c) -> p j c", c=2)
        PE.after(t_silu[0], t_silu[1], t_zero)
        mm(psum[b][:, 0:48 * 2], zero, ident[:, 0:96], start=True, stop=False, skip_group_check=True)
        first = START[name]
        with nc.tensor.Fori(0, NADA // SLOTS) as i:
            for s in range(SLOTS):
                arrive(first + s, i)
                w = slot(first + s)
                rhs = cond[:, bass.ds(i * (2 * SLOTS) + 2 * s, cols)]
                for j in range(48):
                    ins = mm(acc[:, j, 0:cols], w[:, j * P:(j + 1) * P], rhs, start=False, stop=False,
                             skip_group_check=True)
                ins.then_inc(freed, 1)
        t = PE.done(mm(psum[b][:, 96:98], ident, ident[:, 0:2], start=False, stop=True, skip_group_check=True))
        DVE.after(t)
        for c in range(cols):
            t = DVE.done(DVE.eng.tensor_tensor(mod[:, :, c], acc[:, :, c], cst(bias), ADD))
        bank.free[b] = t
        return t

    def rstd_of(src, blocks, n, width, dst, sq, *toks):
        SC.after(*toks)
        t = SC.done(SC.eng.activation(sq, src, ACT.Square))
        b = bank.next()
        PE.after(t)
        t = PE.done(product(psum[b][:, 0:n], [(ones, sq[:, k, :]) for k in range(blocks)]))
        SC.after(t)
        t = SC.done(SC.eng.activation(dst, psum[b][:, 0:n], ACT.Sqrt, bias=eps, scale=1.0 / width))
        bank.free[b] = t
        DVE.after(t)
        return DVE.done(DVE.eng.reciprocal(dst, dst))

    def normed(src, dst, norm, shift, scale, col, *toks):
        mark = take.at
        sq = take(KB * T).rearrange("p (k t) -> p k t", k=KB)
        rstd = take(T)
        if scale is not None:
            DVE.after(*toks)
            tg = DVE.done(DVE.eng.scalar_tensor_tensor(gain[:, :, col], mod[:, scale * KB:(scale + 1) * KB, col], 1.0,
                                                       cst(norm), ADD, MUL))
        else:
            tg = None
        t = rstd_of(src, KB, T, D, rstd, sq, *toks)
        DVE.after(t, tg)
        t = DVE.done(DVE.eng.tensor_tensor(dst, src, rep(rstd, KB), MUL))
        DVE.after(t)
        SC.after(t)
        for k in range(KB):
            if scale is None:
                t = DVE.done(DVE.eng.tensor_scalar(dst[:, k, :], dst[:, k, :], cst(norm)[:, k:k + 1], None, MUL))
            elif k % 2:
                t = DVE.done(DVE.eng.tensor_scalar(dst[:, k, :], dst[:, k, :], gain[:, k, col:col + 1],
                                                   mod[:, shift * KB + k, col:col + 1], MUL, ADD))
            else:
                ta = SC.done(SC.eng.activation(dst[:, k, :], dst[:, k, :], ACT.Identity,
                                               scale=gain[:, k, col:col + 1],
                                               bias=mod[:, shift * KB + k, col:col + 1]))
        take.at = mark
        return (t, None if scale is None else ta)

    def residual(feats, tile_of, gate, *toks):
        PE.after(*toks)
        for j in range(KB):
            tile, c = tile_of(j)
            if j == 0 or tile_of(j - 1)[0] != tile:
                arrive(tile)
            b = bank.next()
            ins = product(psum[b][:, 0:T], [(proj(tile)[:, k, c:c + P], feats[:, k, :]) for k in range(KB)])
            t = PE.done(ins)
            if j == KB - 1 or tile_of(j + 1)[0] != tile:
                free_tile(1)
            DVE.after(t)
            t = DVE.done(DVE.eng.scalar_tensor_tensor(x[:, j, :], psum[b][:, 0:T], mod[:, gate * KB + j, 0:1],
                                                      x[:, j, :], MUL, ADD))
            bank.free[b] = t
        return t

    def free_tile(n):
        PE.after(PE.last()).sem_inc(freed, n)

    up_done, act_done, prod_done, down_done = (nc.alloc_semaphore(n) for n in
                                               ("ffn_up", "ffn_silu", "ffn_product", "ffn_down"))
    BASE = 8
    ffn_base = [BASE]
    GP.eng.sem_inc(prod_done, BASE)
    GP.eng.sem_inc(down_done, BASE)
    GP.eng.sem_inc(up_done, BASE)
    GP.eng.sem_inc(act_done, BASE)

    def ffn(name, h, ntiles, gate, gates=None):
        phase()
        bank.free = [None] * 8
        mark = take.at
        sil = take(4 * T).rearrange("p (n t) -> p n t", n=4)
        hid = take(4 * T).rearrange("p (n t) -> p n t", n=4)
        first, base = START[name], ffn_base[0]
        dbase = BASE + (base - BASE) // 2
        ffn_base[0] += 2 * ntiles
        for b in range(4, 8):
            mm(psum[b], zero, par[:, 0:512], start=True, stop=False, skip_group_check=True)

        def plus(v, i, k):
            return v if i is None else v + i * k

        def up(n, i=None):
            arrive(first + n, i)
            w = slot(first + n)
            for b in range(2):
                m = 2 * n + b
                nc.tensor.wait_ge(prod_done, plus(base + m - 3, i, 2 * SLOTS))
                pb = psum[m % 4]
                for half in range(2):
                    wg = w[:, half * 2048:(half + 1) * 2048].rearrange("p (k n) -> p k n", k=KB)
                    for k in range(KB):
                        ins = mm(pb[:, half * T:(half + 1) * T], wg[:, k, b * P:(b + 1) * P], h[:, k, :],
                                 start=k == 0, stop=k == KB - 1)
                ins.then_inc(up_done, 1)

        def down(n, i=None):
            w = slot(first + n)[:, 4096:].rearrange("p (b n) -> p b n", b=2)
            for b in range(2):
                m = 2 * n + b
                nc.tensor.wait_ge(prod_done, plus(base + m + 1, i, 2 * SLOTS))
                for j in range(KB):
                    ins = mm(psum[4 + j // 2][:, (j % 2) * T:(j % 2 + 1) * T], w[:, b, j * P:(j + 1) * P],
                             hid[:, m % 4, :], start=False, stop=False, skip_group_check=True)
            ins.then_inc(down_done, 1)
            nc.tensor.wait_ge(down_done, plus(dbase + n + 1, i, SLOTS))
            nc.tensor.sem_inc(freed, 1)

        def act(n, i=None):
            for b in range(2):
                m = 2 * n + b
                nc.scalar.wait_ge(up_done, plus(base + m + 1, i, 2 * SLOTS))
                nc.scalar.wait_ge(prod_done, plus(base + m - 3, i, 2 * SLOTS))
                nc.scalar.activation(sil[:, m % 4, :], psum[m % 4][:, 0:T], ACT.Silu).then_inc(act_done, 1)

        def prod(n, i=None):
            for b in range(2):
                m = 2 * n + b
                nc.vector.wait_ge(act_done, plus(base + m + 1, i, 2 * SLOTS))
                nc.vector.wait_ge(down_done, plus(dbase + n - 1, i, SLOTS))
                ins = nc.vector.tensor_tensor(hid[:, m % 4, :], sil[:, m % 4, :], psum[m % 4][:, T:2 * T], MUL)
                if gates is None:
                    ins.then_inc(prod_done, 1)
                else:
                    ins.then_inc(gated, 1)
                    gcount = (m + 1) if i is None else (i * (2 * SLOTS) + (m + 1))
                    nc.vector.wait_ge(gated, gcount)
                    e = n // 2
                    g = gates[:, e, :] if i is None else gates_flat[:, bass.ds(i * (SLOTS // 2 * T) + e * T, T)]
                    nc.vector.tensor_tensor(hid[:, m % 4, :], hid[:, m % 4, :], g, MUL).then_inc(prod_done, 1)

        if gates is not None:
            gated = nc.alloc_semaphore("gated")
            gates_flat = gates.rearrange("p e t -> p (e t)")
        loops = (ntiles - 1) // SLOTS
        up(0)
        with nc.tensor.Fori(0, loops) as i:
            for n in range(SLOTS):
                up(n + 1, i)
                down(n, i)
        for n in range(loops * SLOTS, ntiles):
            if n + 1 < ntiles:
                up(n + 1)
            down(n)
        with nc.scalar.Fori(0, loops) as i:
            for n in range(SLOTS):
                act(n, i)
        with nc.vector.Fori(0, loops) as i:
            for n in range(SLOTS):
                prod(n, i)
        for n in range(loops * SLOTS, ntiles):
            act(n)
            prod(n)
        nc.vector.wait_ge(down_done, dbase + ntiles)
        for j in range(KB):
            t = DVE.done(DVE.eng.scalar_tensor_tensor(x[:, j, :], psum[4 + j // 2][:, (j % 2) * T:(j % 2 + 1) * T],
                                                      mod[:, gate * KB + j, 0:1], x[:, j, :], MUL, ADD))
        take.at = mark
        phase()
        return t

    saved = nc.alloc_semaphore("saved")

    def finish(src, dst, *toks):
        phase()
        nc.gpsimd.dma_start(dst, src).then_inc(saved, 16)
        nc.gpsimd.wait_ge(saved, 16)

    t_mod = modulation("ada0", silu_c[0], "ada_b0", 2)
    hA_buf = take(KB * TT)
    hA = hA_buf.rearrange("p (k t) -> p k t", k=KB)
    mark0 = take.at
    cx = take(KB * T).rearrange("p (k t) -> p k t", k=KB)
    ctx_in = nc.alloc_semaphore("context_loaded")
    nc.gpsimd.dma_start(cx, ctx1).then_inc(ctx_in, 16)
    tc_ = normed(cx, hA[:, :, 0:T], "norm_mix0", 0, 1, 1, t_mod, (ctx_in, 16, "ctx_in"))
    tl = normed(x, hA[:, :, T:TT], "norm_mix0", 0, 1, 0, t_mod, tc_[0], tc_[1])
    PE.after(*tc_, *tl)
    phase()
    take.at = mark0

    qkv_buf = take(4 * T + TT + NT * P)
    qT = qkv_buf[:, 0:4 * T].rearrange("p (j t) -> p j t", j=4)
    kT = qkv_buf[:, 4 * T:4 * T + TT]
    v = qkv_buf[:, 4 * T + TT:].rearrange("p (n c) -> p n c", n=NT)
    xp_buf = take(6 * 2 * 258)
    xp = xp_buf.rearrange("p (b g t) -> p b g t", b=6, g=2)
    zs = take(4 * T).rearrange("p (j t) -> p j t", j=4)
    dt = take(NT * 16)
    feats = take(KB * T).rearrange("p (k t) -> p k t", k=KB)
    t_pad = GP.done(GP.eng.memset(xp, 0.0))
    hy = START["hy"]

    def block_rows(tile, c, n0, n1):
        return [(proj(tile)[:, k, c:c + P], hA[:, k, n0:n1]) for k in range(KB)]

    arrive(hy)
    for j in range(4):
        b = bank.next()
        t = PE.done(product(psum[b][:, 0:T], block_rows(hy, j * P, T, TT)))
        SC.after(t)
        bank.free[b] = SC.done(SC.eng.copy(qT[:, j, :], psum[b][:, 0:T]))
    b = bank.next()
    t = PE.done(product(psum[b], block_rows(hy, 4 * P, 0, TT)))
    DVE.after(t)
    bank.free[b] = DVE.done(DVE.eng.tensor_copy(kT, psum[b]))
    b = bank.next()
    for n in range(NT):
        ins = product(psum[b][:, n * P:(n + 1) * P], [(hA[:, k, n * P:(n + 1) * P], proj(hy)[:, k, 5 * P:6 * P])
                                                      for k in range(KB)])
    t = PE.done(ins)
    DVE.after(t)
    t_v = bank.free[b] = DVE.done(DVE.eng.tensor_copy(v, psum[b]))
    t_qk = (SC.last(), DVE.last())
    free_tile(1)
    arrive(hy + 1)
    for j in range(6):
        b = bank.next()
        n0 = T if j == 5 else 0
        t = PE.done(product(psum[b][:, n0:TT], block_rows(hy + 1, j * P, n0, TT)))
        SC.after(t, t_pad)
        for g in range(n0 // T, 2):
            bank.free[b] = SC.done(SC.eng.copy(xp[:, j, g, 1:T + 1], psum[b][:, g * T:(g + 1) * T]))
    t_xp = SC.last()
    free_tile(1)
    b = bank.next()
    for n in range(NT):
        ins = product(psum[b][:, n * 16:(n + 1) * 16],
                      [(hA[:, k, n * P:(n + 1) * P], cst("w_dt")[:, k * 16:(k + 1) * 16]) for k in range(KB)])
    t = PE.done(ins)
    DVE.after(t)
    dt3 = dt.rearrange("p (n c) -> p n c", n=NT)
    t_dt = bank.free[b] = DVE.done(DVE.eng.tensor_tensor(dt3, psum[b][:, 0:64].rearrange("p (n c) -> p n c", n=NT),
                                                         rep(cst("dt_bias"), NT), ADD))
    arrive(hy + 2)
    for j in range(4):
        b = bank.next()
        t = PE.done(product(psum[b][:, 0:T], block_rows(hy + 2, j * P, T, TT)))
        SC.after(t)
        t_z = bank.free[b] = SC.done(SC.eng.activation(zs[:, j, :], psum[b][:, 0:T], ACT.Silu))

    mark1 = take.at
    phase()
    sq = take(4 * T).rearrange("p (j t) -> p j t", j=4)
    rs = take(4 * T)

    def head_norm(src, ncols, weight, out_, *toks):
        SC.after(*toks)
        t = SC.done(SC.eng.activation(sq.rearrange("p j t -> p (j t)")[:, 0:ncols], src, ACT.Square))
        for c in range(0, ncols, 512):
            b = bank.next()
            PE.after(t)
            t1 = PE.done(mm(psum[b], cst("pair"), sq.rearrange("p j t -> p (j t)")[:, c:c + 512]))
            SC.after(t1)
            t2 = bank.free[b] = SC.done(SC.eng.activation(rs[:, c:c + 512], psum[b], ACT.Sqrt, bias=eps,
                                                          scale=1.0 / 64))
        DVE.after(t2)
        t = DVE.done(DVE.eng.reciprocal(rs[:, 0:ncols], rs[:, 0:ncols]))
        DVE.after(t)
        t = DVE.done(DVE.eng.scalar_tensor_tensor(out_, src, cst(weight), rs[:, 0:ncols], MUL, MUL))
        return t

    qflat = qT.rearrange("p j t -> p (j t)")
    t_q = head_norm(qflat, 4 * T, "qn", qflat, *t_qk)
    t_k = head_norm(kT, TT, "kn", kT, t_q)
    rq = take(5 * T)

    def rope(vec, o, t0):
        b = bank.next()
        PE.after(t0)
        t = PE.done(mm(psum[b][:, 0:T], cst("rot"), vec))
        DVE.after(t)
        t1 = bank.free[b] = DVE.done(DVE.eng.tensor_tensor(o, psum[b][:, 0:T], cst("sin"), MUL))
        t2 = DVE.done(DVE.eng.tensor_tensor(vec, vec, cst("cos"), MUL))
        DVE.after(t2)
        return DVE.done(DVE.eng.tensor_tensor(vec, vec, o, ADD))

    for j in range(4):
        t_q = rope(qT[:, j, :], rq[:, j * T:(j + 1) * T], t_k)
    t_k = rope(kT[:, T:TT], rq[:, 4 * T:5 * T], t_k)

    prob = [take(TT) for _ in range(2)]
    probT = [take(TT) for _ in range(2)]
    stat = tiny(16 * 3).rearrange("p (u c) -> p u c", c=3)
    t_pv = [None, None]
    t_pT = [None, None]
    scale = 64 ** -0.5
    PE.after(t_q, t_k, t_v)
    unit = 0
    for j in range(4):
        for half in range(2):
            hp = slice(64 * half, 64 * half + 64)
            bo = bank.next()
            for n in range(2):
                u = unit % 2
                st = stat[:, unit, :]
                b = bank.next()
                t = PE.done(mm(psum[b], qT[hp, j, n * P:(n + 1) * P], kT[hp, :]))
                DVE.after(t)
                t = DVE.done(DVE.eng.reduce_max(st[:, 0:1], psum[b], AX.X))
                DVE.after(t)
                t = DVE.done(DVE.eng.tensor_scalar(st[:, 0:1], st[:, 0:1], -scale, None, MUL))
                SC.after(t, t_pT[u])
                t = bank.free[b] = SC.done(SC.eng.activation(prob[u], psum[b], ACT.Exp, bias=st[:, 0:1], scale=scale,
                                                             accum_out=st[:, 1:2]))
                DVE.after(t)
                t = DVE.done(DVE.eng.reciprocal(st[:, 2:3], st[:, 1:2]))
                DVE.after(t)
                t = DVE.done(DVE.eng.tensor_scalar(prob[u], prob[u], st[:, 2:3], None, MUL))
                PE.after(t)
                b = bank.next()
                for i in range(NT):
                    ins = nc.tensor.transpose(psum[b][:, i * P:(i + 1) * P], prob[u][:, i * P:(i + 1) * P], ident)
                t = t_pT[u] = PE.done(ins)
                DVE.after(t, t_pv[u])
                t = bank.free[b] = DVE.done(DVE.eng.tensor_copy(probT[u], psum[b]))
                PE.after(t)
                ins = product(psum[bo][hp, n * P:(n + 1) * P], [(v[:, i, hp], probT[u][:, i * P:(i + 1) * P])
                                                                 for i in range(NT)])
                t_pv[u] = PE.done(ins)
                unit += 1
            SC.after(t_pv[0], t_pv[1])
            bank.free[bo] = SC.done(SC.eng.copy(feats[hp, j, :], psum[bo][hp, 0:T]))
    phase()
    take.at = mark1

    in_hA = Carve(hA_buf, KB * TT)
    xc = in_hA(6 * TT).rearrange("p (b t) -> p b t", b=6)
    for j in range(6):
        g0 = 1 if j == 5 else 0
        acc = xc[:, j, :].rearrange("p (g t) -> p g t", g=2)[:, g0:2, :]
        cw = cst("conv_w")[:, 3 * j:3 * j + 3]
        DVE.after(t_xp)
        t = DVE.done(DVE.eng.tensor_scalar(acc, xp[:, j, g0:2, 0:T], cw[:, 0:1], None, MUL))
        for tap in (1, 2):
            DVE.after(t)
            t = DVE.done(DVE.eng.scalar_tensor_tensor(acc, xp[:, j, g0:2, tap:tap + T], cw[:, tap:tap + 1], acc,
                                                      MUL, ADD))
        SC.after(t)
        t_xc = SC.done(SC.eng.activation(acc, acc, ACT.Silu, bias=cst("conv_b")[:, j:j + 1]))
    xs = take(NT * 512).rearrange("p (n c) -> p n c", n=NT)
    Bn = take(NT * P).rearrange("p (n c) -> p n c", n=NT)
    PE.after(t_xc)
    for n in range(NT):
        b = bank.next()
        for j in range(4):
            ins = nc.tensor.transpose(psum[b][:, j * P:(j + 1) * P], xc[:, j, n * P:(n + 1) * P], ident)
        t = PE.done(ins)
        DVE.after(t)
        t_xs = bank.free[b] = DVE.done(DVE.eng.tensor_copy(xs[:, n, :], psum[b]))
    b = bank.next()
    for n in range(NT):
        ins = nc.tensor.transpose(psum[b][:, n * P:(n + 1) * P], xc[:, 4, n * P:(n + 1) * P], ident)
    t = PE.done(ins)
    DVE.after(t)
    t_Bn = bank.free[b] = DVE.done(DVE.eng.tensor_copy(Bn, psum[b]))

    def softplus(val, n, *toks):
        mark = tiny.at
        u, z, z2, p = (tiny(n) for _ in range(4))
        SC.after(*toks)
        t = SC.done(SC.eng.activation(u, val, ACT.Abs))
        SC.after(t)
        t = SC.done(SC.eng.activation(u, u, ACT.Exp, scale=-1.0))

        def step(tok, f):
            DVE.after(tok)
            return DVE.done(f(DVE.eng))
        t = step(t, lambda e: e.tensor_scalar(z, u, 2.0, None, ADD))
        t = step(t, lambda e: e.reciprocal(z, z))
        t = step(t, lambda e: e.tensor_tensor(z, z, u, MUL))
        t = step(t, lambda e: e.tensor_tensor(z2, z, z, MUL))
        t = step(t, lambda e: e.tensor_scalar(p, z2, 2.0 / 17, None, MUL))
        for k in (15, 13, 11, 9, 7, 5, 3):
            t = step(t, lambda e: e.scalar_tensor_tensor(p, p, 2.0 / k, z2, ADD, MUL))
        t = step(t, lambda e: e.scalar_tensor_tensor(p, p, 2.0, z, ADD, MUL))
        t = step(t, lambda e: e.scalar_tensor_tensor(val, val, 0.0, p, ALU.max, ADD))
        tiny.at = mark
        return t

    dtA, wend, etot = (take(NT * 16) for _ in range(3))
    na = tiny(16)
    t = softplus(dt, NT * 16, t_dt)
    t1 = SC.done(SC.eng.activation(na, cst("a_log"), ACT.Exp))
    DVE.after(t1, t)
    v3 = lambda a: a.rearrange("p (n c) -> p n c", n=NT)
    t_dtA = t = DVE.done(DVE.eng.scalar_tensor_tensor(v3(dtA), v3(dt), -1.0, rep(na, NT), MUL, MUL))
    PE.after(t)
    b = bank.next()
    for i, lhs in enumerate((after_[0], after_[1], ones)):
        ins = mm(psum[b][:, i * 64:(i + 1) * 64], lhs, dtA)
    t = PE.done(ins)
    SC.after(t)
    for d in range(2):
        SC.done(SC.eng.activation(v3(wend)[:, :, 8 * d:8 * d + 8],
                                  v3(psum[b][:, d * 64:(d + 1) * 64])[:, :, 8 * d:8 * d + 8], ACT.Exp))
    t = bank.free[b] = SC.done(SC.eng.activation(etot, psum[b][:, 128:192], ACT.Exp))
    DVE.after(t)
    t_wend = DVE.done(DVE.eng.tensor_tensor(wend, wend, dt, MUL))

    order = ((0, 1, 2, 3), (1, 0, 3, 2))
    H = [[in_hA(256).rearrange("p (e c) -> p e c", e=4) for _ in range(2)] for _ in range(2)]
    xw = [take(512).rearrange("p (h c) -> p h c", h=8) for _ in range(2)]
    t_H = [[None, None], [None, None]]
    t_use = [None, None]
    t_last = [None, None]
    for i in range(3):
        for d in range(2):
            n = order[d][i]
            DVE.after(t_wend, t_xs, t_use[d])
            t = DVE.done(DVE.eng.tensor_tensor(xw[d], xs[:, n, :].rearrange("p (h c) -> p h c", h=8),
                                               bc(v3(wend)[:, n, 8 * d:8 * d + 8], 64), MUL))
            PE.after(t, t_Bn)
            b = bank.next()
            t = t_use[d] = PE.done(mm(psum[b], Bn[:, n, :], xw[d].rearrange("p h c -> p (h c)")))
            src, dst = H[d][max(i - 1, 0) if i < 2 else 0], H[d][0 if i < 2 else 1]
            for g in range(2):
                pp = slice(64 * g, 64 * g + 64)
                new = psum[b][pp, g * 256:(g + 1) * 256].rearrange("p (e c) -> p e c", e=4)
                DVE.after(t)
                if i == 0:
                    t1 = DVE.done(DVE.eng.tensor_copy(dst[pp], new))
                else:
                    DVE.after(t_last[d])
                    t1 = DVE.done(DVE.eng.tensor_tensor(dst[pp], src[pp],
                                                        bc(v3(etot)[pp, n, 8 * d + 4 * g:8 * d + 4 * g + 4], 64), MUL))
                    DVE.after(t1)
                    t1 = DVE.done(DVE.eng.tensor_tensor(dst[pp], dst[pp], new, ADD))
            bank.free[b] = t1
            t_last[d] = t1
    t_H = DVE.last()

    phase()
    in_xp, in_qkv = Carve(xp_buf, 6 * 2 * 258), Carve(qkv_buf, 4 * T + TT + NT * P)
    y = in_xp(4 * T).rearrange("p (j t) -> p j t", j=4)
    xdt = [in_xp(512).rearrange("p (h c) -> p h c", h=8) for _ in range(2)]
    L = [in_qkv(1024).rearrange("p (h c) -> p h c", h=8) for _ in range(2)]
    M = [take(1024).rearrange("p (h c) -> p h c", h=8) for _ in range(2)]
    CE = [in_xp(512).rearrange("p (e c) -> p e c", e=4) for _ in range(2)]
    G = [xw[d].rearrange("p h c -> p (h c)").rearrange("p (e g c) -> p e g c", e=4, g=2) for d in range(2)]
    CB = [tiny(256).rearrange("p (g c) -> p g c", g=2) for _ in range(2)]
    t_y = None
    for n in (2, 3):
        cols = slice(n * P, (n + 1) * P)
        ready = []
        for d in range(2):
            dA = v3(dtA)[:, n, 8 * d:8 * d + 8]
            DVE.after(t_dtA, t_y)
            t = DVE.done(DVE.eng.tensor_tensor(xdt[d], xs[:, n, :].rearrange("p (h c) -> p h c", h=8),
                                               bc(v3(dt)[:, n, 8 * d:8 * d + 8], 64), MUL))
            t_L = DVE.done(DVE.eng.tensor_tensor(L[d], rep(after_[d], 8), bc(dA, P), MUL))
            for g in range(2):
                t_G = DVE.done(DVE.eng.tensor_copy(G[d][:, :, g, :], bc(dA[:, 4 * g:4 * g + 4], 64)))
            PE.after(t_L, t_G)
            for half in range(2):
                b = bank.next()
                for h in range(4):
                    ins = mm(psum[b][:, h * P:(h + 1) * P], L[d][:, 4 * half + h, :], tri[d])
                t = PE.done(ins)
                SC.after(t, t_y)
                t_M = bank.free[b] = SC.done(SC.eng.activation(
                    M[d][:, 4 * half:4 * half + 4, :].rearrange("p h c -> p (h c)"), psum[b], ACT.Exp))
            for g in range(2):
                pp = slice(64 * g, 64 * g + 64)
                b = bank.next()
                t = PE.done(mm(psum[b][:, 0:P], xc[pp, 4, cols], xc[pp, 5, cols]))
                DVE.after(t)
                t = bank.free[b] = DVE.done(DVE.eng.tensor_tensor(CB[d][:, g, :], psum[b][:, 0:P], tri[d], MUL))
            DVE.after(t, t_M)
            for g in range(2):
                t_M = DVE.done(DVE.eng.tensor_tensor(M[d][:, 4 * g:4 * g + 4, :], M[d][:, 4 * g:4 * g + 4, :],
                                                     rep(CB[d][:, g, :], 4), MUL))
            b = bank.next()
            for e in range(4):
                ins = mm(psum[b][:, e * P:(e + 1) * P], G[d][:, e, :, :].rearrange("p g c -> p (g c)"), tri[d])
            t = PE.done(ins)
            SC.after(t, t_y)
            t = bank.free[b] = SC.done(SC.eng.activation(CE[d].rearrange("p e c -> p (e c)"), psum[b], ACT.Exp))
            DVE.after(t)
            t = DVE.done(DVE.eng.tensor_tensor(CE[d], CE[d], rep(xc[:, 5, cols], 4), MUL))
            ready += [t_M, t]
        PE.after(t_H, *ready)
        yb = [bank.next(), bank.next()]
        for h in range(8):
            g, e, pp = h // 4, h % 4, slice(64 * (h // 4), 64 * (h // 4) + 64)
            pairs = []
            for d in range(2):
                pairs += [(xdt[d][:, h, :], M[d][:, h, :]),
                          (H[d][order[d].index(n) - 2][pp, e, :], CE[d][pp, e, :])]
            ins = product(psum[yb[g]][64 * (h % 2):64 * (h % 2) + 64, (e // 2) * P:(e // 2 + 1) * P], pairs)
        t = t_y = PE.done(ins)
        DVE.after(t)
        for j in range(4):
            t = DVE.done(DVE.eng.scalar_tensor_tensor(y[:, j, cols.start - T:cols.stop - T], xc[:, j, cols],
                                                      cst("d_skip")[:, j:j + 1],
                                                      psum[yb[j // 2]][:, (j % 2) * P:(j % 2 + 1) * P],
                                                      MUL, ADD))
        bank.free[yb[0]] = bank.free[yb[1]] = t
    DVE.after(t)
    t = DVE.done(DVE.eng.tensor_tensor(y, y, zs, MUL))
    phase()
    in_qkv = Carve(qkv_buf, 4 * T + TT + NT * P)
    sq = in_qkv(4 * T).rearrange("p (j t) -> p j t", j=4)
    rs = in_qkv(2 * T).rearrange("p (g t) -> p g t", g=2)
    for g in range(2):
        t1 = rstd_of(y[:, 2 * g:2 * g + 2, :], 2, T, 256, rs[:, g, :], sq[:, 2 * g:2 * g + 2, :], t)
        DVE.after(t1)
        for j in (2 * g, 2 * g + 1):
            t2 = DVE.done(DVE.eng.scalar_tensor_tensor(feats[:, 4 + j, :], y[:, j, :], cst("ssm_norm")[:, j:j + 1],
                                                       rs[:, g, :], MUL, MUL))
    residual(feats, lambda j: (hy + 2, (4 + j) * P) if j < 2 else (hy + 3, (j - 2) * P), 2, t2)
    phase()

    take.at = 0
    h = take(KB * T).rearrange("p (k t) -> p k t", k=KB)
    normed(x, h, "norm_ffn0", 3, 4, 0, DVE.last())
    ffn("ffn0", h, NFFN, 5)

    t_mod = modulation("ada1", silu_c[0], "ada_b1", 1)
    tl = normed(x, h, "norm_mix1", 0, 1, 0, t_mod)
    phase()
    mark1 = take.at
    cu = take(KB * 258).rearrange("p (k t) -> p k t", k=KB)
    gb = take(KB * T).rearrange("p (k t) -> p k t", k=KB)
    gc = take(KB * T).rearrange("p (k t) -> p k t", k=KB)
    t_pad = GP.done(GP.eng.memset(cu, 0.0))
    sc = START["sc"]
    for i in range(4):
        arrive(sc + i)
        for jj in range(2):
            j = 2 * i + jj
            banks = [bank.next() for _ in range(3)]
            for part in range(3):
                c = (3 * jj + part) * P
                ins = product(psum[banks[part]][:, 0:T], [(proj(sc + i)[:, k, c:c + P], h[:, k, :]) for k in range(KB)])
            t = PE.done(ins)
            SC.after(t)
            bank.free[banks[0]] = SC.done(SC.eng.copy(gb[:, j, :], psum[banks[0]][:, 0:T]))
            t1 = bank.free[banks[1]] = SC.done(SC.eng.copy(gc[:, j, :], psum[banks[1]][:, 0:T]))
            DVE.after(t1, t_pad)
            t = bank.free[banks[2]] = DVE.done(DVE.eng.tensor_tensor(cu[:, j, 1:T + 1], gc[:, j, :],
                                                                     psum[banks[2]][:, 0:T], MUL))
            DVE.after(t)
            cw = cst("sc_conv")[:, 3 * j:3 * j + 3]
            t = DVE.done(DVE.eng.tensor_scalar(gc[:, j, :], cu[:, j, 0:T], cw[:, 0:1], None, MUL))
            for tap in (1, 2):
                DVE.after(t)
                t = DVE.done(DVE.eng.scalar_tensor_tensor(gc[:, j, :], cu[:, j, tap:tap + T], cw[:, tap:tap + 1],
                                                          gc[:, j, :], MUL, ADD))
            DVE.after(t)
            t = DVE.done(DVE.eng.tensor_tensor(gb[:, j, :], gb[:, j, :], gc[:, j, :], MUL))
        free_tile(1)
    residual(gb, lambda j: (sc + 4, j * P) if j < TB else (sc + 5, (j - TB) * P), 2, t)
    phase()
    take.at = mark1
    normed(x, h, "norm_ffn1", 3, 4, 0, DVE.last())
    ffn("ffn1", h, NFFN, 5)
    normed(x, x, "final1", None, None, 0, DVE.last())
    phase()

    phase()
    bank.free = [None] * 8
    take.at = 0
    t_mod = modulation("mod2", silu_c[1], "mod_b2", 2)
    feats = take(KB * T).rearrange("p (k t) -> p k t", k=KB)
    mark_feats = take.at
    hA_buf = take(KB * TT)
    hA = hA_buf.rearrange("p (k t) -> p k t", k=KB)
    mark0 = take.at
    cx = take(KB * T).rearrange("p (k t) -> p k t", k=KB)
    nc.gpsimd.dma_start(cx, ctx2).then_inc(ctx_in, 16)
    tc_ = normed(cx, hA[:, :, 0:T], "norm1_2", 0, 1, 1, t_mod, (ctx_in, 32, "ctx_in"))
    normed(x, hA[:, :, T:TT], "norm1_2", 0, 1, 0, *tc_)
    phase()
    take.at = mark0
    in2 = START["in2"]
    ba = tiny(NT * 16)
    ba3 = v3(ba)
    b = bank.next()
    for n in range(NT):
        ins = product(psum[b][:, n * 16:(n + 1) * 16],
                      [(hA[:, k, n * P:(n + 1) * P], cst("w_ba")[:, k * 16:(k + 1) * 16]) for k in range(KB)])
    t = PE.done(ins)
    DVE.after(t)
    t_ba = bank.free[b] = DVE.done(DVE.eng.tensor_copy(ba, psum[b][:, 0:64]))

    HH = 4
    zs2 = take(4 * T).rearrange("p (j t) -> p j t", j=4)
    qh = take(4 * T).rearrange("p (j t) -> p j t", j=4)
    vh = take(2 * 512).rearrange("p (n c) -> p n c", n=2)
    kh = take(2 * 1024).rearrange("p (n c) -> p n c", n=2)
    lf = take(2 * 1024).rearrange("p (n c) -> p n c", n=2)
    Sh = [[take(512) for _ in range(2)] for _ in range(2)]
    E = [take(1024).rearrange("p (l t) -> p l t", l=8) for _ in range(2)]
    kT2 = take(2 * P).rearrange("p (d t) -> p d t", d=2)
    ksum = take(P)
    att = take(P)
    kd = [E[d].rearrange("p l t -> p (l t)")[:, 0:512] for d in range(2)]
    eth = [tiny(4) for _ in range(2)]

    def gates_natural(tok0):
        for c in range(6):
            tile, cc = in2 + c // 3, (c % 3) * 256
            if tok0 == 0 and c % 3 == 0:
                arrive(tile)
            b = bank.next()
            for n in range(2):
                ins = product(psum[b][:, n * 256:(n + 1) * 256],
                              [(hA[:, k, (tok0 + n) * P:(tok0 + n + 1) * P], proj(tile)[:, k, cc:cc + 256])
                               for k in range(KB)])
            t = PE.done(ins)
            raw = psum[b].rearrange("p (n c) -> p n c", n=2)
            if c < 2:
                SC.after(t)
                bank.free[b] = SC.done(SC.eng.copy(vh[:, :, c * 256:(c + 1) * 256], raw))
                continue
            l, k_ = lf[:, :, (c - 2) * 256:(c - 1) * 256], kh[:, :, (c - 2) * 256:(c - 1) * 256]
            SC.after(t)
            t1 = SC.done(SC.eng.activation(l, raw, ACT.Abs))
            SC.after(t1)
            t1 = SC.done(SC.eng.activation(l, l, ACT.Exp, scale=-1.0))
            SC.after(t1)
            t1 = SC.done(SC.eng.activation(k_, l, ACT.Ln, bias=1.0))
            DVE.after(t1)
            t1 = DVE.done(DVE.eng.tensor_scalar(l, raw, 0.0, None, ALU.min))
            DVE.after(t1)
            t1 = DVE.done(DVE.eng.tensor_tensor(l, l, k_, SUB))
            DVE.after(t1)
            t1 = bank.free[b] = DVE.done(DVE.eng.tensor_tensor(k_, l, raw, SUB))
            SC.after(t1)
            SC.done(SC.eng.activation(k_, k_, ACT.Exp))
        return SC.last(), DVE.last()

    def hg_state(d, n, src, dst, *toks):
        f = lf[:, n, d * 512:(d + 1) * 512]
        b = bank.next()
        PE.after(*toks)
        t = PE.done(mm(psum[b], after_[d], f))
        SC.after(t)
        t = bank.free[b] = SC.done(SC.eng.activation(kd[d], psum[b], ACT.Exp))
        DVE.after(t)
        t_kd = DVE.done(DVE.eng.tensor_tensor(kd[d], kd[d], kh[:, n, d * 512:(d + 1) * 512], MUL))
        b = bank.next()
        for h in range(HH):
            ins = mm(psum[b][:, h:h + 1], f[:, h * P:(h + 1) * P], ones[:, 0:1])
        t = PE.done(ins)
        SC.after(t)
        t_e = bank.free[b] = SC.done(SC.eng.activation(eth[d], psum[b][:, 0:4], ACT.Exp))
        PE.after(t_kd)
        b = bank.next()
        for h in range(HH):
            ins = mm(psum[b][:, h * P:(h + 1) * P], kd[d][:, h * P:(h + 1) * P], vh[:, n, h * P:(h + 1) * P])
        t = PE.done(ins)
        DVE.after(t, t_e)
        if src is None:
            t = DVE.done(DVE.eng.tensor_copy(dst, psum[b]))
        else:
            h4 = lambda a: a.rearrange("p (h e) -> p h e", h=HH)
            t = DVE.done(DVE.eng.tensor_tensor(h4(dst), h4(src), bc(eth[d], P), MUL))
            DVE.after(t)
            t = DVE.done(DVE.eng.tensor_tensor(dst, dst, psum[b], ADD))
        bank.free[b] = t
        return t

    toks = gates_natural(0)
    for i in range(2):
        for d in range(2):
            hg_state(d, order[d][i], None if i == 0 else Sh[d][0], Sh[d][0], *toks, DVE.last(), SC.last())
    phase()
    toks = gates_natural(2)
    free_tile(2)
    for part in range(2):
        arrive(in2 + 2 + part)
        for j in range(TB):
            o = part * TB + j
            b = bank.next()
            t = PE.done(product(psum[b][:, 0:T], block_rows(in2 + 2 + part, j * P, T, TT)))
            SC.after(t)
            dst = (qh, feats[:, 0:4, :], zs2)[o // 4][:, o % 4, :]
            bank.free[b] = SC.done(SC.eng.activation(dst, psum[b][:, 0:T], ACT.Silu))
        free_tile(1)
    t_q = SC.last()
    gsil = feats[:, 0:4, :]
    for d in range(2):
        t = hg_state(d, order[d][2] - 2, Sh[d][0], Sh[d][1], *toks, DVE.last())
    phase()

    mask = (cst("maskF"), cst("maskB"))
    spans = (cst("spanF"), cst("spanB"))
    t_free = None
    for n in range(2):
        cols = slice(n * P, (n + 1) * P)
        for h in range(HH):
            q = qh[:, h, cols]
            b = bank.next()
            for d in range(2):
                ins = nc.tensor.transpose(psum[b][:, d * P:(d + 1) * P], kh[:, n, d * 512 + h * P:d * 512 + (h + 1) * P],
                                          ident)
            t = PE.done(ins)
            DVE.after(t, t_free)
            t_kT = DVE.done(DVE.eng.tensor_copy(kT2.rearrange("p d t -> p (d t)"), psum[b][:, 0:256]))
            bank.free[b] = t_kT
            DVE.after(t_kT)
            t_ks = DVE.done(DVE.eng.tensor_tensor(ksum, kT2[:, 0, :], kT2[:, 1, :], ADD))
            ba_ = bank.next()
            PE.after(t_ks)
            t = PE.done(mm(psum[ba_][:, 0:P], ksum, q))
            DVE.after(t)
            t_att = bank.free[ba_] = DVE.done(DVE.eng.tensor_tensor(att, psum[ba_][:, 0:P], ident, MUL))
            for d in range(2):
                f = lf[:, n, d * 512 + h * P:d * 512 + (h + 1) * P]
                Ef = E[d].rearrange("p l t -> p (l t)")
                for half in range(2):
                    b = bank.next()
                    t = PE.done(mm(psum[b], f, spans[d][:, half * 512:(half + 1) * 512]))
                    SC.after(t, t_free)
                    t_E = bank.free[b] = SC.done(SC.eng.activation(Ef[:, half * 512:(half + 1) * 512], psum[b],
                                                                   ACT.Exp))
                DVE.after(t_E, t_kT)
                GP.after(t_E, t_kT)
                for li, lev in enumerate(LEVELS):
                    Ev = E[d][:, li, :].rearrange("p (m s c) -> p m s c", s=2, c=lev)
                    qv = q.rearrange("p (m s c) -> p m s c", s=2, c=lev)
                    kv = kT2[:, d, :].rearrange("p (m s c) -> p m s c", s=2, c=lev)
                    tq, ts = (1, 0) if d == 0 else (0, 1)
                    t1 = DVE.done(DVE.eng.tensor_tensor(Ev[:, :, tq, :], Ev[:, :, tq, :], qv[:, :, tq, :], MUL))
                    t2 = GP.done(GP.eng.tensor_tensor(Ev[:, :, ts, :], Ev[:, :, ts, :], kv[:, :, ts, :], MUL))
                t_qd = DVE.done(DVE.eng.tensor_tensor(E[d][:, 7, :], E[d][:, 7, :], q, MUL))
                PE.after(t1, t2, t_qd)
                for l0, l1 in ((0, 4), (4, 7)):
                    b = bank.next()
                    for li in range(l0, l1):
                        ins = mm(psum[b][:, (li - l0) * P:(li - l0 + 1) * P], E[d][:, li, :], E[d][:, li, :])
                    t = PE.done(ins)
                    for li in range(l0, l1):
                        DVE.after(t, t_att)
                        t_att = DVE.done(DVE.eng.copy_predicated(att, mask[d][:, li * P:(li + 1) * P].bitcast(U32),
                                                                 psum[b][:, (li - l0) * P:(li - l0 + 1) * P]))
                    bank.free[b] = t_att
            PE.after(t_att, t_q)
            b = bank.next()
            hs = slice(h * P, (h + 1) * P)
            t = t_free = PE.done(product(psum[b][:, 0:P],
                                         [(vh[:, n, hs], att),
                                          (Sh[0][n][:, hs], E[0][:, 7, :]), (Sh[1][1 - n][:, hs], E[1][:, 7, :])]))
            SC.after(t)
            bank.free[b] = SC.done(SC.eng.copy(q, psum[b][:, 0:P]))

    def head_gate(o, gate, weight, out_):
        phase()
        mark = take.at
        sq = take(4 * T).rearrange("p (j t) -> p j t", j=4)
        rs = take(4 * T).rearrange("p (j t) -> p j t", j=4)
        t = SC.done(SC.eng.activation(sq, o, ACT.Square))
        for g in range(2):
            b = bank.next()
            PE.after(t)
            t1 = PE.done(mm(psum[b], ones, sq[:, 2 * g:2 * g + 2, :].rearrange("p j t -> p (j t)")))
            SC.after(t1)
            t2 = bank.free[b] = SC.done(SC.eng.activation(rs[:, 2 * g:2 * g + 2, :].rearrange("p j t -> p (j t)"),
                                                          psum[b], ACT.Sqrt, bias=eps, scale=1.0 / P))
        DVE.after(t2)
        t = DVE.done(DVE.eng.reciprocal(rs, rs))
        DVE.after(t)
        fl = lambda a: a.rearrange("p j t -> p (j t)")
        t = DVE.done(DVE.eng.scalar_tensor_tensor(fl(rs), fl(o), cst(weight), fl(rs), MUL, MUL))
        DVE.after(t)
        t = DVE.done(DVE.eng.tensor_tensor(out_, rs, gate, MUL))
        phase()
        take.at = mark

    phase()
    in_hg = Carve(lf.rearrange("p n c -> p (n c)"), 2048)
    saved_take, take = take, in_hg
    head_gate(qh, gsil, "hg_norm", feats[:, 0:4, :])
    take = saved_take

    take.at = mark0 + 4 * T
    dq = take(4 * T).rearrange("p (j t) -> p j t", j=4)
    dk = take(4 * TT).rearrange("p (j t) -> p j t", j=4)
    kn = take(NT * 512).rearrange("p (n c) -> p n c", n=NT)
    vn = take(NT * 512).rearrange("p (n c) -> p n c", n=NT)
    GW = 64
    GR = T // GW
    pads = [take((GR + 2) * (GW + 2) + T + 2) for _ in range(2)]
    dvt = [take(TT) for _ in range(2)]
    for p_ in pads:
        t_pad = GP.done(GP.eng.memset(p_, 0.0))
    t_used = [None, None]
    t_tr = [None, None]
    for o in range(12):
        tile = in2 + 4 + o // TB
        if o % TB == 0:
            arrive(tile)
        j, u = o % 4, o % 2
        n0 = T if o < 4 else 0
        b = bank.next()
        t = PE.done(product(psum[b][:, n0:TT], block_rows(tile, (o % TB) * P, n0, TT)))
        if o % TB == TB - 1:
            free_tile(1)
        grid = pads[u][:, 0:(GR + 2) * (GW + 2)].rearrange("p (r c) -> p r c", r=GR + 2)
        line = pads[u][:, (GR + 2) * (GW + 2):]
        SC.after(t, t_used[u], t_pad)
        t = SC.done(SC.eng.copy(grid[:, 1:GR + 1, 1:GW + 1], psum[b][:, T:TT].rearrange("p (r c) -> p r c", r=GR)))
        if o >= 4:
            t = SC.done(SC.eng.copy(line[:, 1:T + 1], psum[b][:, 0:T]))
        bank.free[b] = t
        dst = dq[:, j, :] if o < 4 else dk[:, j, :] if o < 8 else dvt[u]
        lat = (dst if o < 4 else dst[:, T:TT])
        lat3 = lat.rearrange("p (r c) -> p r c", r=GR)
        cw = cst("dn_conv")[:, 9 * o:9 * o + 9]
        DVE.after(t, t_tr[u])
        for tap in range(9):
            src = grid[:, tap // 3:tap // 3 + GR, tap % 3:tap % 3 + GW]
            if tap == 0:
                t = DVE.done(DVE.eng.tensor_scalar(lat3, src, cw[:, 0:1], None, MUL))
            else:
                t = DVE.done(DVE.eng.scalar_tensor_tensor(lat3, src, cw[:, tap:tap + 1], lat3, MUL, ADD))
            DVE.after(t)
        if o >= 4:
            for tap in range(3):
                src = line[:, tap:tap + T]
                if tap == 0:
                    t = DVE.done(DVE.eng.tensor_scalar(dst[:, 0:T], src, cw[:, 3:4], None, MUL))
                else:
                    t = DVE.done(DVE.eng.scalar_tensor_tensor(dst[:, 0:T], src, cw[:, 3 + tap:4 + tap], dst[:, 0:T],
                                                              MUL, ADD))
                DVE.after(t)
        t_used[u] = t
        SC.after(t)
        t = SC.done(SC.eng.activation(dst, dst, ACT.Silu))
        if o >= 8:
            PE.after(t)
            b = bank.next()
            for n in range(NT):
                ins = nc.tensor.transpose(psum[b][:, n * P:(n + 1) * P], dvt[u][:, n * P:(n + 1) * P], ident)
            t = t_tr[u] = PE.done(ins)
            SC.after(t)
            bank.free[b] = SC.done(SC.eng.copy(vn[:, :, j * P:(j + 1) * P],
                                               psum[b].rearrange("p (n c) -> p n c", n=NT)))
    phase()
    in_hA = Carve(hA_buf, KB * TT)
    sq = in_hA(512)
    rsn = in_hA(512)
    for i in range(6):
        src = (dq[:, 2 * i:2 * i + 2, :] if i < 2 else dk[:, i - 2:i - 1, :]).rearrange("p j t -> p (j t)")
        SC.after(DVE.last(), PE.last())
        t = SC.done(SC.eng.activation(sq, src, ACT.Square))
        PE.after(t)
        b = bank.next()
        t = PE.done(mm(psum[b], ones, sq))
        SC.after(t)
        t = bank.free[b] = SC.done(SC.eng.activation(rsn, psum[b], ACT.Sqrt, bias=eps))
        DVE.after(t)
        t = DVE.done(DVE.eng.reciprocal(rsn, rsn))
        DVE.after(t)
        t = DVE.done(DVE.eng.scalar_tensor_tensor(src, src, P ** -0.5 if i < 2 else 1.0, rsn, MUL, MUL))
    PE.after(t)
    for n in range(NT):
        b = bank.next()
        for h in range(HH):
            ins = nc.tensor.transpose(psum[b][:, h * P:(h + 1) * P], dk[:, h, n * P:(n + 1) * P], ident)
        t = PE.done(ins)
        SC.after(t)
        bank.free[b] = SC.done(SC.eng.copy(kn[:, n, :], psum[b]))

    beta, la, ecum, ekd, etd = (tiny(NT * 8) for _ in range(5))
    b8 = lambda a: a.rearrange("p (n c) -> p n c", n=NT)
    SC.after(t_ba)
    t = SC.done(SC.eng.activation(b8(beta), ba3[:, :, 0:8], ACT.Exp, scale=-1.0))
    DVE.after(t)
    t = DVE.done(DVE.eng.tensor_scalar(beta, beta, 1.0, None, ADD))
    DVE.after(t)
    t = DVE.done(DVE.eng.reciprocal(beta, beta))
    t = DVE.done(DVE.eng.tensor_tensor(b8(la), ba3[:, :, 8:16], rep(cst("dn_dtb"), NT), ADD))
    t = softplus(la, NT * 8, t)
    na8 = tiny(8)
    SC.after(t)
    t1 = SC.done(SC.eng.activation(na8, cst("dn_alog"), ACT.Exp))
    DVE.after(t, t1)
    t = DVE.done(DVE.eng.scalar_tensor_tensor(b8(la), b8(la), -1.0, rep(na8, NT), MUL, MUL))
    PE.after(t)
    b = bank.next()
    for i, lhs in enumerate((tri[0], tri[1], after_[0], after_[1], ones)):
        ins = mm(psum[b][:, i * 32:(i + 1) * 32], lhs, la)
    t = PE.done(ins)
    SC.after(t)
    for d in range(2):
        hd = slice(4 * d, 4 * d + 4)
        SC.done(SC.eng.activation(b8(ecum)[:, :, hd], b8(psum[b][:, d * 32:(d + 1) * 32])[:, :, hd], ACT.Exp))
        SC.done(SC.eng.activation(b8(ekd)[:, :, hd], b8(psum[b][:, (2 + d) * 32:(3 + d) * 32])[:, :, hd], ACT.Exp))
    bank.free[b] = SC.done(SC.eng.activation(etd, psum[b][:, 128:160], ACT.Exp))
    phase()

    in_hA = Carve(hA_buf, KB * TT)
    take.at = mark0 + 4 * T + 4 * T + 4 * TT + 2 * NT * 512
    pool2 = [in_hA(512) for _ in range(8)]
    NTm, Tm, TTm, Zm = ([pool2[2 * i + d] for d in range(2)] for i in range(4))
    Dm = [take(512) for _ in range(2)]
    S = [take(512) for _ in range(2)]
    RH = [take(512) for _ in range(2)]
    kdc = [take(512) for _ in range(2)]
    h4 = lambda a: a.rearrange("p (h c) -> p h c", h=HH)
    od = feats[:, 4:8, :]
    strict = (after_[1], after_[0])

    def heads_mm(b, f, *toks):
        PE.after(*toks)
        for h in range(HH):
            a, c = f(h)
            ins = mm(psum[b][:, h * P:(h + 1) * P], a, c)
        return PE.done(ins)

    for step in range(4):
        phase()
        ns = [order[d][step] for d in range(2)]
        ready = [None, None]
        for d in range(2):
            n = ns[d]
            cols = slice(n * P, (n + 1) * P)
            dl = b8(la)[:, n, 4 * d:4 * d + 4]
            db = b8(beta)[:, n, 4 * d:4 * d + 4]
            t_L = DVE.done(DVE.eng.tensor_tensor(h4(Zm[d]), rep(after_[d], HH), bc(dl, P), MUL))
            b = bank.next()
            t = heads_mm(b, lambda h: (h4(Zm[d])[:, h, :], tri[d]), t_L)
            SC.after(t)
            t_D = bank.free[b] = SC.done(SC.eng.activation(Dm[d], psum[b], ACT.Exp))
            b = bank.next()
            t = heads_mm(b, lambda h: (db[:, h:h + 1].broadcast_to([P, P]), ident))
            DVE.after(t)
            t_kb = bank.free[b] = DVE.done(DVE.eng.tensor_tensor(h4(Tm[d]), h4(psum[b]), dk[:, :, cols], MUL))
            b = bank.next()
            t = heads_mm(b, lambda h: (dk[:, h, cols], h4(Tm[d])[:, h, :]), t_kb)
            DVE.after(t, t_D)
            t = bank.free[b] = DVE.done(DVE.eng.tensor_tensor(NTm[d], psum[b], Dm[d], MUL))
            DVE.after(t)
            t = DVE.done(DVE.eng.tensor_tensor(h4(NTm[d]), h4(NTm[d]), rep(strict[d], HH), MUL))
            DVE.after(t)
            for m in (Tm, TTm):
                t = DVE.done(DVE.eng.tensor_copy(h4(m[d]), rep(ident, HH)))
            ready[d] = t
        for li in range(len(LEVELS)):
            for d in range(2):
                b = bank.next()
                t = heads_mm(b, lambda h: (h4(NTm[d])[:, h, :], h4(Tm[d])[:, h, :]), ready[d])
                DVE.after(t)
                t = bank.free[b] = DVE.done(DVE.eng.tensor_tensor(
                    h4(Zm[d]), h4(psum[b]), rep(mask[1 - d][:, li * P:(li + 1) * P], HH), MUL))
                b1, b2 = bank.next(), bank.next()
                t1 = heads_mm(b1, lambda h: (h4(TTm[d])[:, h, :], h4(Zm[d])[:, h, :]), t)
                t2 = heads_mm(b2, lambda h: (h4(Zm[d])[:, h, :], h4(TTm[d])[:, h, :]))
                DVE.after(t2)
                bank.free[b1] = DVE.done(DVE.eng.tensor_tensor(Tm[d], Tm[d], psum[b1], SUB))
                ready[d] = bank.free[b2] = DVE.done(DVE.eng.tensor_tensor(TTm[d], TTm[d], psum[b2], SUB))
        for d in range(2):
            n = ns[d]
            cols = slice(n * P, (n + 1) * P)
            col = lambda a: b8(a)[:, n, 4 * d:4 * d + 4]
            if step == 0:
                DVE.after(ready[d])
                t = DVE.done(DVE.eng.tensor_tensor(h4(RH[d]), h4(vn[:, n, :]), bc(col(beta), P), MUL))
            else:
                b = bank.next()
                t = heads_mm(b, lambda h: (dk[:, h, cols], h4(S[d])[:, h, :]), ready[d])
                DVE.after(t)
                t = bank.free[b] = DVE.done(DVE.eng.tensor_tensor(h4(RH[d]), h4(psum[b]), bc(col(ecum), P), MUL))
                DVE.after(t)
                t = DVE.done(DVE.eng.tensor_tensor(RH[d], vn[:, n, :], RH[d], SUB))
                DVE.after(t)
                t = DVE.done(DVE.eng.tensor_tensor(h4(RH[d]), h4(RH[d]), bc(col(beta), P), MUL))
            b = bank.next()
            t = heads_mm(b, lambda h: (h4(TTm[d])[:, h, :], h4(RH[d])[:, h, :]), t)
            SC.after(t)
            vnew = Zm[d]
            t_v = bank.free[b] = SC.done(SC.eng.copy(vnew, psum[b]))
            if step >= 2:
                lat = slice(cols.start - T, cols.stop - T)
                DVE.after(PE.last())
                t = DVE.done(DVE.eng.tensor_tensor(h4(Dm[d]), h4(Dm[d]), rep(tri[d], HH), MUL))
                b = bank.next()
                t1 = heads_mm(b, lambda h: (dk[:, h, cols], dq[:, h, lat]))
                DVE.after(t, t1)
                t_qk = bank.free[b] = DVE.done(DVE.eng.tensor_tensor(Dm[d], Dm[d], psum[b], MUL))
                b = bank.next()
                t = heads_mm(b, lambda h: (col(la)[:, h:h + 1].broadcast_to([P, P]), tri[d]))
                SC.after(t)
                t = bank.free[b] = SC.done(SC.eng.activation(Tm[d], psum[b], ACT.Exp))
                DVE.after(t)
                t_qd = DVE.done(DVE.eng.tensor_tensor(h4(Tm[d]), h4(Tm[d]), dq[:, :, lat], MUL))
                b = bank.next()
                PE.after(t_v, t_qk, t_qd)
                for h in range(HH):
                    ins = product(psum[b][:, h * P:(h + 1) * P],
                                  [(h4(vnew)[:, h, :], h4(Dm[d])[:, h, :]), (h4(S[d])[:, h, :], h4(Tm[d])[:, h, :])])
                t = PE.done(ins)
                DVE.after(t)
                if step == 2:
                    t = DVE.done(DVE.eng.tensor_copy(od[:, :, lat], h4(psum[b])))
                else:
                    t = DVE.done(DVE.eng.tensor_tensor(od[:, :, lat], od[:, :, lat], h4(psum[b]), ADD))
                bank.free[b] = t
            if step < 3:
                t = DVE.done(DVE.eng.tensor_tensor(h4(kdc[d]), h4(kn[:, n, :]), bc(col(ekd), P), MUL))
                b = bank.next()
                t = heads_mm(b, lambda h: (h4(kdc[d])[:, h, :], h4(vnew)[:, h, :]), t, t_v)
                DVE.after(t)
                if step == 0:
                    t = DVE.done(DVE.eng.tensor_copy(S[d], psum[b]))
                else:
                    t = DVE.done(DVE.eng.tensor_tensor(h4(S[d]), h4(S[d]), bc(col(etd), P), MUL))
                    DVE.after(t)
                    t = DVE.done(DVE.eng.tensor_tensor(S[d], S[d], psum[b], ADD))
                bank.free[b] = t
    phase()
    take.at = mark0 + 4 * T
    head_gate(od, zs2, "dn_norm", od)
    out2 = START["out2"]
    residual(feats, lambda j: (out2, j * P) if j < TB else (out2 + 1, (j - TB) * P), 2)
    phase()
    take.at = 0
    h = take(KB * T).rearrange("p (k t) -> p k t", k=KB)
    normed(x, h, "norm2_2", 3, 4, 0, DVE.last())
    phase()
    gbc = take(EXPERTS * T).rearrange("p (e t) -> p e t", e=EXPERTS)
    mark_t = tiny.at
    tiny.at = 128
    lg = tiny(40).rearrange("p (n c) -> p n c", n=2)
    b = bank.next()
    for n in range(2):
        ins = product(psum[b][:, n * 20:(n + 1) * 20],
                      [(h[:, k, n * P:(n + 1) * P], cst("w_rt")[:, k * 20:(k + 1) * 20]) for k in range(KB)])
    t = PE.done(ins)
    DVE.after(t)
    t = bank.free[b] = DVE.done(DVE.eng.tensor_tensor(lg, psum[b][:, 0:40].rearrange("p (n c) -> p n c", n=2),
                                                      rep(cst("b_rt"), 2), ADD))

    def vec(f, *toks):
        DVE.after(DVE.last(), *toks)
        return DVE.done(f(DVE.eng))

    def pick(src):
        m, eq, m2 = tiny(2), tiny(8), tiny(2)
        eq = eq.rearrange("p (n c) -> p n c", n=2)
        vec(lambda e: e.tensor_reduce(m, src, AX.X, ALU.max))
        vec(lambda e: e.tensor_tensor(eq, src, bc(m, 4), ALU.is_equal))
        vec(lambda e: e.tensor_tensor(eq, eq, rep(cst("first4"), 2), MUL))
        vec(lambda e: e.tensor_reduce(m2, eq, AX.X, ALU.max))
        vec(lambda e: e.tensor_tensor(eq, eq, bc(m2, 4), ALU.is_equal))
        return m, eq

    n4 = lambda: tiny(8).rearrange("p (n c) -> p n c", n=2)
    gl = lg[:, :, 0:4]
    gm, goh = pick(gl)
    ex, gw = n4(), tiny(2)
    t = vec(lambda e: e.tensor_tensor(ex, gl, bc(gm, 4), SUB))
    SC.after(t)
    t = SC.done(SC.eng.activation(ex, ex, ACT.Exp))
    vec(lambda e: e.tensor_reduce(gw, ex, AX.X, ADD), t)
    vec(lambda e: e.reciprocal(gw, gw))
    el, es = tiny(32).rearrange("p (n e g) -> p n e g", n=2, e=4), n4()
    for n in range(2):
        vec(lambda e: e.tensor_tensor(el[:, n], lg[:, n, 4:20].rearrange("p (g e) -> p e g", g=4),
                                      rep(goh[:, n, :], 4), MUL))
    vec(lambda e: e.tensor_reduce(es.rearrange("p n c -> p (n c)"), el.rearrange("p n e g -> p (n e) g"), AX.X, ADD))
    v1, oh1 = pick(es)
    rest = n4()
    vec(lambda e: e.scalar_tensor_tensor(rest, oh1, -1e30, es, MUL, ADD))
    v2, oh2 = pick(rest)
    e2, w1, w2_ = tiny(2), tiny(2), tiny(2)
    t = vec(lambda e: e.tensor_tensor(e2, v2, v1, SUB))
    SC.after(t)
    t = SC.done(SC.eng.activation(e2, e2, ACT.Exp))
    vec(lambda e: e.tensor_scalar(w1, e2, 1.0, None, ADD), t)
    vec(lambda e: e.reciprocal(w1, w1))
    vec(lambda e: e.tensor_tensor(w1, w1, gw, MUL))
    vec(lambda e: e.tensor_tensor(w2_, w1, e2, MUL))
    vec(lambda e: e.tensor_tensor(oh1, oh1, bc(w1, 4), MUL))
    vec(lambda e: e.tensor_tensor(oh2, oh2, bc(w2_, 4), MUL))
    vec(lambda e: e.tensor_tensor(oh1, oh1, oh2, ADD))
    gt = tiny(32).rearrange("p (n g e) -> p n g e", n=2, g=4)
    for n in range(2):
        t = vec(lambda e: e.tensor_tensor(gt[:, n], bc(goh[:, n, :], 4), rep(oh1[:, n, :], 4), MUL))
    PE.after(t)
    for e_ in range(0, EXPERTS, 2):
        b = bank.next()
        for ee in range(2):
            for n in range(2):
                g_ = gt[:, n, (e_ + ee) // 4, (e_ + ee) % 4:(e_ + ee) % 4 + 1]
                ins = mm(psum[b][:, (2 * ee + n) * P:(2 * ee + n + 1) * P], g_.broadcast_to([P, P]), ident)
        t = PE.done(ins)
        SC.after(t)
        bank.free[b] = SC.done(SC.eng.copy(gbc[:, e_:e_ + 2, :].rearrange("p e t -> p (e t)"), psum[b]))
    ffn("moe", h, NMOE, 5, gates=gbc)
    normed(x, x, "final2", None, None, 0, DVE.last())
    finish(x, out)


def _host(inputs):
    f = np.float32
    g = {k: np.asarray(a) for k, a in inputs.items()}

    def kblocks(w):
        return w.reshape(w.shape[0] // P, P, w.shape[1]).transpose(1, 0, 2)

    def tiles(w):
        return [kblocks(w[:, a:a + TC]).reshape(P, TILE) for a in range(0, w.shape[1], TC)]

    def pad(w):
        n = -w.shape[1] % TC
        return np.concatenate([w, np.zeros((w.shape[0], n), f)], 1) if n else w

    def ada(w):
        return [w[k * P:(k + 1) * P] for k in range(KB)]

    def ffn(wg, wu, wd):
        out = []
        for a in range(0, wg.shape[1], GROUP):
            out.append(np.concatenate([kblocks(wg[:, a:a + GROUP]).reshape(P, -1),
                                       kblocks(wu[:, a:a + GROUP]).reshape(P, -1),
                                       kblocks(wd[a:a + GROUP]).reshape(P, -1)], 1))
        return out

    q = 512
    win, wout = g["hy_w_in"][0], g["hy_w_out"][0]
    heads = [j + 4 * half for j in range(4) for half in range(2)]
    qcols = np.concatenate([np.arange(64 * h, 64 * h + 64) for h in heads])
    wq, wkv, wz, wxbc, wdt = win[:, qcols], win[:, q:q + 256], win[:, 768:1280], win[:, 1280:2048], win[:, 2048:]
    wo = np.concatenate([wout[qcols], wout[q:]], 0)
    hy = tiles(np.concatenate([wq, wkv, wxbc, wz, wo], 1))
    scw = g["sc_w_in"][0].reshape(D, 3, KB, P)
    sc = tiles(scw.transpose(0, 2, 1, 3).reshape(D, 3 * D)) + tiles(pad(g["sc_w_out"][0]))
    w2 = g["w_in_2"][0]
    W = 512
    part = {n: w2[:, W * i:W * i + W] for i, n in enumerate(("q", "i", "g", "ff", "fb", "dq", "dk", "dv", "dz"))}
    in2 = tiles(np.concatenate([part[n] for n in ("i", "ff", "fb", "q", "g", "dz", "dq", "dk", "dv")], 1))
    parts = {
        "ada0": ada(g["ada_w"][0]), "hy": hy,
        "ffn0": ffn(g["ffn_w_gate"][0], g["ffn_w_up"][0], g["ffn_w_down"][0]),
        "ada1": ada(g["ada_w"][1]), "sc": sc,
        "ffn1": ffn(g["ffn_w_gate"][1], g["ffn_w_up"][1], g["ffn_w_down"][1]),
        "mod2": ada(g["w_mod_2"][0]), "in2": in2, "out2": tiles(pad(g["w_out_2"][0])),
        "moe": [t for e in range(EXPERTS) for t in ffn(g["w_gate_2"][0, e], g["w_up_2"][0, e], g["w_down_2"][0, e])],
    }
    stream = np.stack([t for n, _ in STREAM for t in parts[n]])
    assert stream.shape == (NTILES, P, TILE)

    i = np.arange(P)
    u, t_ = i[:, None], i[None, :]
    col = lambda a: np.ascontiguousarray(a.reshape(-1, P).T)
    row = lambda a: np.broadcast_to(a.reshape(1, -1), (P, a.size))

    def span(d):
        out = []
        for h in LEVELS:
            mid = t_ // (2 * h) * (2 * h) + h
            right, left = t_ >= mid, t_ < mid
            if d == 0:
                out.append((right & (u >= mid) & (u <= t_)) | (left & (u > t_) & (u < mid)))
            else:
                out.append((left & (u >= t_) & (u < mid)) | (right & (u >= mid) & (u < t_)))
        out.append(u <= t_ if d == 0 else u >= t_)
        return np.concatenate(out, 1)

    def level_masks():
        return [(u // (2 * h) == t_ // (2 * h)) & (u % (2 * h) < h) & (t_ % (2 * h) >= h) for h in LEVELS]

    masks = level_masks()
    rot = np.zeros((P, P), f)
    rot[i[0::2], i[1::2]] = 1
    rot[i[1::2], i[0::2]] = -1
    tok = np.arange(T)
    inv = (1.0 / (f(10000.0) ** (np.arange(0, 32, 2, dtype=f) / f(32)))).astype(f)
    ang = np.concatenate([(tok // 64).astype(f)[:, None] * inv, (tok % 64).astype(f)[:, None] * inv], 1).T
    ang = ang[(i % 64) // 2]
    cols = {
        "ident": np.eye(P), "triF": u <= t_, "triB": u >= t_, "afterF": u > t_, "afterB": u < t_,
        "ones": np.ones((P, P)), "pair": u // 64 == t_ // 64, "rot": rot, "cos": np.cos(ang), "sin": np.sin(ang),
        "spanF": span(0), "spanB": span(1), "maskF": np.concatenate(masks, 1),
        "maskB": np.concatenate([m.T for m in masks], 1),
        "c": np.stack([col(g["c"][0]), col(g["c_ctx"])], 2).reshape(P, -1),
        "c2": np.stack([col(g["c_2"][0]), col(g["c_ctx_2"])], 2).reshape(P, -1),
        "ada_b0": col(g["ada_b"][0]), "ada_b1": col(g["ada_b"][1]), "mod_b2": col(g["b_mod_2"][0]),
        "norm_mix0": col(g["norm_mix"][0]), "norm_mix1": col(g["norm_mix"][1]),
        "norm_ffn0": col(g["norm_ffn"][0]), "norm_ffn1": col(g["norm_ffn"][1]), "final1": col(g["final_norm"]),
        "norm1_2": col(g["norm1_w_2"][0]), "norm2_2": col(g["norm2_w_2"][0]), "final2": col(g["final_norm_w_2"]),
        "qn": np.tile(g["hy_q_norm"][0], 2)[:, None], "kn": np.tile(g["hy_k_norm"][0], 2)[:, None],
        "eps": np.full((P, 1), EPS),
        "conv_w": g["hy_conv_w"][0].reshape(3, 6, P).transpose(2, 1, 0).reshape(P, -1),
        "conv_b": col(g["hy_conv_b"][0]), "dt_bias": row(g["hy_dt_bias"][0]), "a_log": row(g["hy_a_log"][0]),
        "d_skip": col(np.repeat(g["hy_d_skip"][0], 64)), "ssm_norm": col(g["hy_ssm_norm"][0]),
        "w_dt": kblocks(wdt).reshape(P, -1),
        "sc_conv": g["sc_conv_w"][0].reshape(3, KB, P).transpose(2, 1, 0).reshape(P, -1),
        "hg_norm": g["hg_norm_w_2"][0][:, None], "dn_norm": g["dn_norm_w_2"][0][:, None],
        "dn_conv": g["dn_conv_w_2"][0].reshape(9, 12, P).transpose(2, 1, 0).reshape(P, -1),
        "dn_alog": row(g["dn_a_log_2"][0]), "dn_dtb": row(g["dn_dt_bias_2"][0]),
        "w_ba": kblocks(w2[:, 9 * W:]).reshape(P, -1),
        "w_rt": kblocks(np.concatenate([g["w_group_2"][0], g["w_expert_2"][0]], 1)).reshape(P, -1),
        "b_rt": row(np.concatenate([g["b_group_2"][0], g["b_expert_2"][0]])),
        "first4": row(np.array([4, 3, 2, 1])),
    }
    params = np.concatenate([np.asarray(cols[n], f).reshape(P, w) for n, w in COLS], 1)

    def tokens(a):
        return np.ascontiguousarray(a[0].T.reshape(KB, P, T).transpose(1, 0, 2))

    return {"stream": stream, "params": params, "xin": tokens(g["x"]), "ctx1": tokens(g["ctx"]),
            "ctx2": tokens(g["ctx_2"])}


def kernel(**inputs):
    import concourse.bacc as bacc
    from concourse import mybir
    from concourse.bass_utils import run_bass_kernel_spmd
    arrays = _host(inputs)
    nc = bacc.Bacc("TRN2", target_bir_lowering=False, num_devices=1)
    aps = {n: nc.dram_tensor(n, a.shape, mybir.dt.float32, kind="ExternalInput").ap() for n, a in arrays.items()}
    out = nc.dram_tensor("out", (P, KB, T), mybir.dt.float32, kind="ExternalOutput").ap()
    build(nc, out=out, **aps)
    r = run_bass_kernel_spmd(nc, [arrays], core_ids=[0])
    return np.ascontiguousarray(r.results[0]["out"].transpose(1, 0, 2).reshape(D, T).T[None])
```

```python
from itertools import chain

import numpy as np

P = 128
D = 1024
KB = D // P
T = 256
TT = 2 * T
NT = TT // P
TILE = 6144
TC = TILE // KB
TB = TC // P
SLOTS = 3
FFN = 2816
EXPERTS, EFF = 16, 512
GROUP = 256
NADA = KB
NFFN = FFN // GROUP
NMOE = EXPERTS * EFF // GROUP
EPS = 1e-6
SMALL = 1472
LEVELS = (1, 2, 4, 8, 16, 32, 64)

STREAM = (("ada0", NADA), ("hy", 3), ("ada1", NADA), ("mod2", NADA), ("hyo", 2), ("ffn0", NFFN), ("sc", 6),
          ("ffn1", NFFN), ("in2", 6), ("out2", 2), ("moe", NMOE))
START, NTILES = {}, 0
for _name, _n in STREAM:
    START[_name] = NTILES
    NTILES += _n

COLS = (("ident", P), ("triF", P), ("triB", P), ("afterF", P), ("afterB", P), ("ones", P), ("pair", P),
        ("rot", P), ("cos", T), ("sin", T), ("spanF", 8 * P), ("spanB", 8 * P), ("maskF", 7 * P), ("maskB", 7 * P),
        ("c", 2 * KB), ("c2", 2 * KB), ("ada_b0", 48), ("ada_b1", 48), ("mod_b2", 48),
        ("norm_mix0", KB), ("norm_mix1", KB), ("norm_ffn0", KB), ("norm_ffn1", KB), ("final1", KB),
        ("norm1_2", KB), ("norm2_2", KB), ("final2", KB),
        ("qn", 1), ("kn", 1), ("eps", 1), ("conv_w", 18), ("conv_b", 6), ("dt_bias", 16), ("a_log", 16),
        ("d_skip", 4), ("ssm_norm", 4), ("w_dt", KB * 16), ("sc_conv", KB * 3),
        ("hg_norm", 1), ("dn_conv", 12 * 9), ("dn_alog", 8), ("dn_dtb", 8), ("dn_norm", 1),
        ("w_ba", KB * 16), ("w_rt", KB * 20), ("b_rt", 20), ("first4", 4))
AT, NCOLS = {}, 0
for _name, _n in COLS:
    AT[_name] = (NCOLS, _n)
    NCOLS += _n


def build(nc, stream, params, xin, ctx1, ctx2, out):
    import concourse.bass as bass
    from concourse import mybir
    F32 = mybir.dt.float32
    U32 = mybir.dt.uint32
    ACT = mybir.ActivationFunctionType
    ALU = mybir.AluOpType
    AX = mybir.AxisListType
    MUL, ADD, SUB = ALU.mult, ALU.add, ALU.subtract

    class Line:

        def __init__(self, eng, name):
            self.eng, self.sem, self.n, self.seen = eng, nc.alloc_semaphore(name), 0, {}

        def after(self, *tokens):
            for tok in tokens:
                if tok is None:
                    continue
                assert tok != "held", "no bank is free"
                sem, val, key = tok
                if val > self.seen.get(key, 0):
                    self.eng.wait_ge(sem, val)
                    self.seen[key] = val
            return self.eng

        def done(self, ins):
            self.n += 1
            ins.then_inc(self.sem, 1)
            return (self.sem, self.n, id(self))

        def last(self):
            return (self.sem, self.n, id(self))

    PE, DVE, SC, GP = (Line(nc.tensor, "pe_done"), Line(nc.vector, "dve_done"), Line(nc.scalar, "act_done"),
                       Line(nc.gpsimd, "pool_done"))
    COMPUTE = (PE, DVE, SC, GP)

    def phase():
        for line in COMPUTE:
            for other in COMPUTE:
                if other.n:
                    line.after(other.last())

    def sb(name, cols):
        return nc.alloc_sbuf_tensor(name, [P, cols], F32)[:, :]

    ring = [sb(f"ring{s}", TILE) for s in range(SLOTS)]
    par = sb("par", NCOLS)
    x = sb("x", KB * T).rearrange("p (k t) -> p k t", k=KB)
    F32R = mybir.dt.float32r
    mods = [sb(f"mod{i}", 48 * 2).rearrange("p (j c) -> p j c", c=2) for i in range(3)]
    mod = mods[0]
    gain = sb("gain", 2 * KB).rearrange("p (k c) -> p k c", c=2)
    silu_c = [sb(f"silu_c{i}", 2 * KB) for i in range(2)]
    small = sb("small", SMALL)
    ARENA = (nc.sbuf_bytes_remaining - 64) // 4
    BELOW = nc.sbuf_base
    arena = sb("arena", ARENA)

    r_at = [EXPERTS * T]

    def split_pair(name, cols):
        pair = []
        for part in ("high", "low"):
            pair.append(nc.alloc_sbuf_tensor_at(f"{name}_{part}", [P, cols], F32R, offset=BELOW + 4 * r_at[0])[:, :])
            r_at[0] += cols
        return pair

    h_r = split_pair("ffn_in", KB * T)
    gu_r = [split_pair(f"gate_up{i}", 2 * KB * P) for i in range(2)]
    dn_r = [split_pair(f"down{i}", D) for i in range(2)]
    hid_r = [split_pair(f"hidden{i}", T) for i in range(3)]
    assert r_at[0] + 6 * T <= ARENA
    psum = [nc.alloc_psum_tensor(f"bank{b}", [P, 512], F32)[:, :] for b in range(8)]

    def cst(name):
        a, n = AT[name]
        return par[:, a:a + n]

    class Carve:

        def __init__(self, buf, size):
            self.buf, self.size, self.at = buf, size, 0

        def __call__(self, cols):
            a = self.at
            self.at += cols
            assert self.at <= self.size, (self.at, self.size)
            return self.buf[:, a:self.at]

    take = Carve(arena, ARENA)
    tiny = Carve(small, SMALL)

    class Bank:
        HELD = "held"

        def __init__(self):
            self.free, self.n, self.among = [None] * 8, 0, range(8)

        def next(self):
            for _ in self.among:
                b = self.among[self.n % len(self.among)]
                self.n += 1
                if self.free[b] != Bank.HELD:
                    break
            PE.after(self.free[b])
            self.free[b] = Bank.HELD
            return b

    bank = Bank()

    def staggered(units, active=2):
        units = iter(units)
        running = []
        while True:
            while len(running) < active:
                unit = next(units, None)
                if unit is None:
                    break
                running.append(unit)
                if next(unit, "end") == "end":
                    running.remove(unit)
            if not running:
                return
            for unit in list(running):
                if next(unit, "end") == "end":
                    running.remove(unit)

    landed = [nc.alloc_semaphore(f"landed{s}") for s in range(SLOTS)]
    freed = [nc.alloc_semaphore(f"freed{s}") for s in range(SLOTS)]
    loaded = nc.alloc_semaphore("inputs_loaded")
    sync = nc.sync

    arrays = ((par, params), (x, xin))
    for dst, src in arrays:
        sync.dma_start(dst, src).then_inc(loaded, 16)
    for s in range(SLOTS):
        sync.dma_start(ring[s], stream[s, :, :]).then_inc(landed[s], 16)

    def fetch(r, s):
        sync.wait_ge(freed[s], r)
        sync.dma_start(ring[s], stream[r * SLOTS + s, :, :]).then_inc(landed[s], 16)

    with sync.Fori(1, NTILES // SLOTS) as r:
        for s in range(SLOTS):
            fetch(r, s)
    for s in range(NTILES % SLOTS):
        fetch(NTILES // SLOTS, s)

    def slot(tile):
        return ring[tile % SLOTS]

    def arrive(tile, i=None, turns=1, eng=nc.tensor):
        val = 16 * (tile // SLOTS + 1)
        eng.wait_ge(landed[tile % SLOTS], val if i is None else val + i * (16 * turns))

    def proj(tile):
        return slot(tile).rearrange("p (k n) -> p k n", k=KB)

    def mm(out_, lhsT, rhs, start=True, stop=True, **kw):
        return nc.tensor.matmul(out_, lhsT, rhs, start=start, stop=stop, **kw)

    def product(out_, pairs):
        for n, (a, b) in enumerate(pairs):
            ins = mm(out_, a, b, start=n == 0, stop=n == len(pairs) - 1)
        return ins

    def bc(ap, n):
        return ap.unsqueeze(2).broadcast_to([ap.shape[0], ap.shape[1], n])

    def rep(ap, n):
        return ap.unsqueeze(1).broadcast_to([ap.shape[0], n, ap.shape[1]])

    IN = (loaded, 32, "in")
    for line in (PE, DVE, SC, GP):
        line.after(IN)

    ident, ones = cst("ident"), cst("ones")
    tri = (cst("triF"), cst("triB"))
    after_ = (cst("afterF"), cst("afterB"))
    eps = cst("eps")

    t_silu = [SC.done(SC.eng.activation(silu_c[i], cst(n), ACT.Silu)) for i, n in enumerate(("c", "c2"))]
    zero = tiny(128)
    t_zero = GP.done(GP.eng.memset(zero, 0.0))

    PIECES = 4
    PC, PX = 6 * D // PIECES, 2 * D // PIECES

    def modulation(name, cond, bias, dst, sums, with_ctx):
        done = [None] * PIECES
        for k in range(NADA):
            tile = START[name] + k
            arrive(tile, eng=nc.vector)
            for q in range(PIECES):
                DVE.after(done[q], *t_silu)
                jobs = [(sums[q][:, 0:PC], q * PC, PC, 0)]
                if with_ctx:
                    jobs.append((sums[q][:, PC:PC + PX], q * PX, PX, 1))
                for acc, a, w, c in jobs:
                    col = cond[:, 2 * k + c:2 * k + c + 1]
                    src = slot(tile)[:, a:a + w]
                    if k == 0:
                        done[q] = DVE.done(DVE.eng.tensor_scalar(acc, src, col, None, MUL))
                    else:
                        done[q] = DVE.done(DVE.eng.scalar_tensor_tensor(acc, src, col, acc, MUL, ADD))
                if q == PIECES - 1:
                    DVE.after(DVE.last()).sem_inc(freed[tile % SLOTS], 1)
                yield
        PE.after(DVE.last())
        for c, w, n in ((0, PC, 48), (1, PX, 16))[:2 if with_ctx else 1]:
            base = PC if c else 0
            for j in range(0, n, 4):
                b = 6 + j // 4 % 2
                PE.after(bank.free[b])
                for jj in range(4):
                    q, a = (j + jj) * P // w, (j + jj) * P % w
                    ins = mm(psum[b][:, jj * P:(jj + 1) * P], sums[q][:, base + a:base + a + P], ones)
                t = PE.done(ins)
                DVE.after(t)
                bank.free[b] = DVE.done(DVE.eng.tensor_tensor(
                    dst[:, j:j + 4, c], psum[b].rearrange("p (j t) -> p j t", j=4)[:, :, 0], cst(bias)[:, j:j + 4], ADD))
                if j % 8 == 4:
                    yield

    def rstd_of(src, blocks, n, width, dst, sq, *toks):
        SC.after(*toks)
        t = SC.done(SC.eng.activation(sq, src, ACT.Square))
        b = bank.next()
        PE.after(t)
        t = PE.done(product(psum[b][:, 0:n], [(ones, sq[:, k, :]) for k in range(blocks)]))
        SC.after(t)
        t = SC.done(SC.eng.activation(dst, psum[b][:, 0:n], ACT.Sqrt, bias=eps, scale=1.0 / width))
        bank.free[b] = t
        DVE.after(t)
        return DVE.done(DVE.eng.reciprocal(dst, dst))

    def normed(src, dst, norm, shift, scale, col, *toks):
        mark = take.at
        sq = take(KB * T).rearrange("p (k t) -> p k t", k=KB)
        rstd = take(T)
        if scale is not None:
            DVE.after(*toks)
            tg = DVE.done(DVE.eng.scalar_tensor_tensor(gain[:, :, col], mod[:, scale * KB:(scale + 1) * KB, col], 1.0,
                                                       cst(norm), ADD, MUL))
        else:
            tg = None
        t = rstd_of(src, KB, T, D, rstd, sq, *toks)
        DVE.after(t, tg)
        t = DVE.done(DVE.eng.tensor_tensor(dst, src, rep(rstd, KB), MUL))
        DVE.after(t)
        SC.after(t)
        for k in range(KB):
            if scale is None:
                t = DVE.done(DVE.eng.tensor_scalar(dst[:, k, :], dst[:, k, :], cst(norm)[:, k:k + 1], None, MUL))
            elif k % 2:
                t = DVE.done(DVE.eng.tensor_scalar(dst[:, k, :], dst[:, k, :], gain[:, k, col:col + 1],
                                                   mod[:, shift * KB + k, col:col + 1], MUL, ADD))
            else:
                ta = SC.done(SC.eng.activation(dst[:, k, :], dst[:, k, :], ACT.Identity,
                                               scale=gain[:, k, col:col + 1],
                                               bias=mod[:, shift * KB + k, col:col + 1]))
        take.at = mark
        return (t, None if scale is None else ta)

    def residual(feats, tile_of, gate, *toks):
        PE.after(*toks)
        for j in range(KB):
            tile, c = tile_of(j)
            if j == 0 or tile_of(j - 1)[0] != tile:
                arrive(tile)
            b = bank.next()
            ins = product(psum[b][:, 0:T], [(proj(tile)[:, k, c:c + P], feats[:, k, :]) for k in range(KB)])
            t = PE.done(ins)
            if j == KB - 1 or tile_of(j + 1)[0] != tile:
                free_tile(tile)
            DVE.after(t)
            t = DVE.done(DVE.eng.scalar_tensor_tensor(x[:, j, :], psum[b][:, 0:T], mod[:, gate * KB + j, 0:1],
                                                      x[:, j, :], MUL, ADD))
            bank.free[b] = t
        return t

    def free_tile(*tiles_):
        PE.after(PE.last())
        for tile in tiles_:
            nc.tensor.sem_inc(freed[tile % SLOTS], 1)

    names = ("gu_high", "gu_split", "dn_high", "dn_split", "ffn_up", "ffn_silu", "ffn_hidden", "ffn_down")
    gu_high, gu_split, dn_high, dn_split, up_done, act_done, hid_done, down_done = (nc.alloc_semaphore(n) for n in names)
    hid_step = nc.alloc_semaphore("hidden_steps")
    BASE = 4
    for sem_ in (gu_high, gu_split, dn_high, dn_split, up_done, act_done, hid_done, down_done):
        GP.eng.sem_inc(sem_, BASE)
    ffn_base = [BASE, 0]

    def ffn(name, h, ntiles, gate, body, gates=None):
        sil = arena[:, r_at[0]:r_at[0] + 3 * T].rearrange("p (n t) -> p n t", n=3)
        raw = arena[:, r_at[0] + 3 * T:r_at[0] + 6 * T].rearrange("p (n t) -> p n t", n=3)
        h2 = h.rearrange("p k t -> p (k t)")
        phase()
        bank.free = [None] * 8
        t = SC.done(SC.eng.copy(h_r[0], h2))
        DVE.after(t)
        t = DVE.done(DVE.eng.tensor_tensor(h_r[1], h2, h_r[0], SUB))
        PE.after(t)
        if gates is not None:
            spread_gates(gates)
            phase()
            gates_flat = gates.rearrange("p e t -> p (e t)")
        hh, hl = (a.rearrange("p (k t) -> p k t", k=KB) for a in h_r)
        first, base, steps0 = START[name], ffn_base[0], ffn_base[1]
        nstep = 2 if gates is None else 3
        blocks = 2 * ntiles
        ffn_base[0] += blocks
        ffn_base[1] += nstep * blocks
        for b in range(4, 8):
            mm(psum[b], zero, par[:, 0:512], start=True, stop=False, skip_group_check=True)

        def at(v, i, k=1):
            return v if i is None else v + i * (2 * body * k)

        def weights(m):
            w = slot(first + m // 2)[:, (m % 2) * 3072:(m % 2 + 1) * 3072]
            return w[:, 0:2048], w[:, 2048:3072]

        def three(out_, w, a, cols, start):
            mm(out_, w[0][:, cols], a[0], start=start, stop=False, skip_group_check=True)
            mm(out_, w[0][:, cols], a[1], start=False, stop=False, skip_group_check=True)
            return mm(out_, w[1][:, cols], a[0], start=False, stop=True, skip_group_check=True)

        def up(m, i):
            nc.tensor.wait_ge(gu_split, at(base + m + 1, i))
            nc.tensor.wait_ge(hid_done, at(base + m - 2, i))
            for half in range(2):
                for k in range(KB):
                    c = (half * KB + k) * P
                    ins = three(psum[m % 3][:, half * T:(half + 1) * T], gu_r[m % 2], (hh[:, k, :], hl[:, k, :]),
                                slice(c, c + P), k == 0)
            ins.then_inc(up_done, 1)

        def down(m, i):
            nc.tensor.wait_ge(dn_split, at(base + m + 1, i))
            nc.tensor.wait_ge(hid_done, at(base + m + 1, i))
            for j in range(KB):
                ins = three(psum[4 + j // 2][:, (j % 2) * T:(j % 2 + 1) * T], dn_r[m % 2], hid_r[m % 3],
                            slice(j * P, (j + 1) * P), False)
            ins.then_inc(down_done, 1)

        def high_gu(m, i):
            if m % 2 == 0:
                arrive(first + m // 2, i, body // SLOTS, nc.scalar)
            nc.scalar.wait_ge(up_done, at(base + m - 1, i))
            nc.scalar.copy(gu_r[m % 2][0], weights(m)[0]).then_inc(gu_high, 1)

        def high_dn(m, i):
            nc.scalar.wait_ge(down_done, at(base + m - 1, i))
            nc.scalar.copy(dn_r[m % 2][0], weights(m)[1]).then_inc(dn_high, 1)

        def silu(m, i):
            nc.scalar.wait_ge(up_done, at(base + m + 1, i))
            nc.scalar.wait_ge(hid_done, at(base + m - 2, i))
            nc.scalar.activation(sil[:, m % 3, :], psum[m % 3][:, 0:T], ACT.Silu).then_inc(act_done, 1)

        def low_gu(m, i):
            nc.vector.wait_ge(gu_high, at(base + m + 1, i))
            nc.vector.tensor_tensor(gu_r[m % 2][1], weights(m)[0], gu_r[m % 2][0], SUB).then_inc(gu_split, 1)

        def low_dn(m, i):
            nc.vector.wait_ge(dn_high, at(base + m + 1, i))
            nc.vector.tensor_tensor(dn_r[m % 2][1], weights(m)[1], dn_r[m % 2][0], SUB).then_inc(dn_split, 1)
            if m % 2:
                nc.vector.wait_ge(dn_split, at(base + m + 1, i))
                nc.vector.sem_inc(freed[(first + m // 2) % SLOTS], 1)

        def hidden(m, i):
            nc.vector.wait_ge(act_done, at(base + m + 1, i))
            nc.vector.wait_ge(down_done, at(base + m - 2, i))
            done = steps0 + nstep * m
            nc.vector.tensor_tensor(raw[:, m % 3, :], sil[:, m % 3, :], psum[m % 3][:, T:2 * T], MUL)\
                .then_inc(hid_step, 1)
            if gates is not None:
                nc.vector.wait_ge(hid_step, at(done + 1, i, nstep))
                e = m // 4
                g = gates[:, e, :] if i is None else gates_flat[:, bass.ds(i * (body // 2 * T) + e * T, T)]
                nc.vector.tensor_tensor(raw[:, m % 3, :], raw[:, m % 3, :], g, MUL).then_inc(hid_step, 1)
            nc.vector.wait_ge(hid_step, at(done + nstep - 1, i, nstep))
            nc.vector.tensor_copy(hid_r[m % 3][0], raw[:, m % 3, :]).then_inc(hid_step, 1)
            nc.vector.wait_ge(hid_step, at(done + nstep, i, nstep))
            nc.vector.tensor_tensor(hid_r[m % 3][1], raw[:, m % 3, :], hid_r[m % 3][0], SUB).then_inc(hid_done, 1)

        def run(engine, ahead, steps):
            loops = (ntiles - 1) // body
            ahead(0, None)
            with engine.Fori(0, loops) as i:
                for m in range(2 * body):
                    ahead(m + 1, i)
                    for f in steps:
                        f(m, i)
            for m in range(loops * 2 * body, blocks):
                if m + 1 < blocks:
                    ahead(m + 1, None)
                for f in steps:
                    f(m, None)

        run(nc.tensor, up, (down,))
        run(nc.scalar, high_gu, (high_dn, silu))
        run(nc.vector, low_gu, (low_dn, hidden))
        nc.vector.wait_ge(down_done, base + blocks)
        for j in range(KB):
            t = DVE.done(DVE.eng.scalar_tensor_tensor(x[:, j, :], psum[4 + j // 2][:, (j % 2) * T:(j % 2 + 1) * T],
                                                      mod[:, gate * KB + j, 0:1], x[:, j, :], MUL, ADD))
        nc.scalar.wait_ge(down_done, base + blocks)
        phase()
        return t

    saved = nc.alloc_semaphore("saved")

    def finish(src, dst, *toks):
        phase()
        nc.gpsimd.dma_start(dst, src).then_inc(saved, 16)
        nc.gpsimd.wait_ge(saved, 16)

    sums = [take(PC + PX) for _ in range(PIECES)]
    for _ in modulation("ada0", silu_c[0], "ada_b0", mods[0], sums, True):
        pass
    t_mod = DVE.last()
    phase()
    take.at = 0
    hA_buf = take(KB * TT)
    hA = hA_buf.rearrange("p (k t) -> p k t", k=KB)
    mark0 = take.at
    cx = take(KB * T).rearrange("p (k t) -> p k t", k=KB)
    ctx_in = nc.alloc_semaphore("context_loaded")
    nc.gpsimd.dma_start(cx, ctx1).then_inc(ctx_in, 16)
    tc_ = normed(cx, hA[:, :, 0:T], "norm_mix0", 0, 1, 1, t_mod, (ctx_in, 16, "ctx_in"))
    tl = normed(x, hA[:, :, T:TT], "norm_mix0", 0, 1, 0, t_mod, tc_[0], tc_[1])
    PE.after(*tc_, *tl)
    phase()
    take.at = mark0

    qkv_buf = take(4 * T + TT + NT * P)
    qT = qkv_buf[:, 0:4 * T].rearrange("p (j t) -> p j t", j=4)
    kT = qkv_buf[:, 4 * T:4 * T + TT]
    v = qkv_buf[:, 4 * T + TT:].rearrange("p (n c) -> p n c", n=NT)
    xp_buf = take(6 * 2 * 258)
    xp = xp_buf.rearrange("p (b g t) -> p b g t", b=6, g=2)
    zs = take(4 * T).rearrange("p (j t) -> p j t", j=4)
    dt = take(NT * 16)
    feats = take(KB * T).rearrange("p (k t) -> p k t", k=KB)
    t_pad = GP.done(GP.eng.memset(xp, 0.0))
    hy = START["hy"]

    def block_rows(tile, c, n0, n1):
        return [(proj(tile)[:, k, c:c + P], hA[:, k, n0:n1]) for k in range(KB)]

    arrive(hy)
    for j in range(4):
        b = bank.next()
        t = PE.done(product(psum[b][:, 0:T], block_rows(hy, j * P, T, TT)))
        SC.after(t)
        bank.free[b] = SC.done(SC.eng.copy(qT[:, j, :], psum[b][:, 0:T]))
    b = bank.next()
    t = PE.done(product(psum[b], block_rows(hy, 4 * P, 0, TT)))
    DVE.after(t)
    bank.free[b] = DVE.done(DVE.eng.tensor_copy(kT, psum[b]))
    b = bank.next()
    for n in range(NT):
        ins = product(psum[b][:, n * P:(n + 1) * P], [(hA[:, k, n * P:(n + 1) * P], proj(hy)[:, k, 5 * P:6 * P])
                                                      for k in range(KB)])
    t = PE.done(ins)
    DVE.after(t)
    t_v = bank.free[b] = DVE.done(DVE.eng.tensor_copy(v, psum[b]))
    t_qk = (SC.last(), DVE.last())
    free_tile(hy)
    arrive(hy + 1)
    for j in range(6):
        b = bank.next()
        n0 = T if j == 5 else 0
        t = PE.done(product(psum[b][:, n0:TT], block_rows(hy + 1, j * P, n0, TT)))
        SC.after(t, t_pad)
        for g in range(n0 // T, 2):
            bank.free[b] = SC.done(SC.eng.copy(xp[:, j, g, 1:T + 1], psum[b][:, g * T:(g + 1) * T]))
    t_xp = SC.last()
    free_tile(hy + 1)
    b = bank.next()
    for n in range(NT):
        ins = product(psum[b][:, n * 16:(n + 1) * 16],
                      [(hA[:, k, n * P:(n + 1) * P], cst("w_dt")[:, k * 16:(k + 1) * 16]) for k in range(KB)])
    t = PE.done(ins)
    DVE.after(t)
    dt3 = dt.rearrange("p (n c) -> p n c", n=NT)
    t_dt = bank.free[b] = DVE.done(DVE.eng.tensor_tensor(dt3, psum[b][:, 0:64].rearrange("p (n c) -> p n c", n=NT),
                                                         rep(cst("dt_bias"), NT), ADD))
    arrive(hy + 2)
    for j in range(4):
        b = bank.next()
        t = PE.done(product(psum[b][:, 0:T], block_rows(hy + 2, j * P, T, TT)))
        SC.after(t)
        t_z = bank.free[b] = SC.done(SC.eng.activation(zs[:, j, :], psum[b][:, 0:T], ACT.Silu))

    free_tile(hy + 2)

    mark1 = take.at
    phase()
    sq = take(4 * T).rearrange("p (j t) -> p j t", j=4)
    rs = take(4 * T)

    def head_norm(src, ncols, weight, out_, *toks):
        SC.after(*toks)
        t = SC.done(SC.eng.activation(sq.rearrange("p j t -> p (j t)")[:, 0:ncols], src, ACT.Square))
        for c in range(0, ncols, 512):
            b = bank.next()
            PE.after(t)
            t1 = PE.done(mm(psum[b], cst("pair"), sq.rearrange("p j t -> p (j t)")[:, c:c + 512]))
            SC.after(t1)
            t2 = bank.free[b] = SC.done(SC.eng.activation(rs[:, c:c + 512], psum[b], ACT.Sqrt, bias=eps,
                                                          scale=1.0 / 64))
        DVE.after(t2)
        t = DVE.done(DVE.eng.reciprocal(rs[:, 0:ncols], rs[:, 0:ncols]))
        DVE.after(t)
        t = DVE.done(DVE.eng.scalar_tensor_tensor(out_, src, cst(weight), rs[:, 0:ncols], MUL, MUL))
        return t

    qflat = qT.rearrange("p j t -> p (j t)")
    t_q = head_norm(qflat, 4 * T, "qn", qflat, *t_qk)
    t_k = head_norm(kT, TT, "kn", kT, t_q)
    rq = take(5 * T)

    def rope(vec, o, t0):
        b = bank.next()
        PE.after(t0)
        t = PE.done(mm(psum[b][:, 0:T], cst("rot"), vec))
        DVE.after(t)
        t1 = bank.free[b] = DVE.done(DVE.eng.tensor_tensor(o, psum[b][:, 0:T], cst("sin"), MUL))
        t2 = DVE.done(DVE.eng.tensor_tensor(vec, vec, cst("cos"), MUL))
        DVE.after(t2)
        return DVE.done(DVE.eng.tensor_tensor(vec, vec, o, ADD))

    for j in range(4):
        t_q = rope(qT[:, j, :], rq[:, j * T:(j + 1) * T], t_k)
    t_k = rope(kT[:, T:TT], rq[:, 4 * T:5 * T], t_k)

    prob = [take(TT) for _ in range(2)]
    probT = [take(TT) for _ in range(2)]
    stat = tiny(16 * 3).rearrange("p (u c) -> p u c", c=3)
    t_pv = [None, None]
    t_pT = [None, None]
    scale = 64 ** -0.5
    PE.after(t_q, t_k, t_v)
    bank.among = range(6)
    in_hA = Carve(hA_buf, KB * TT)
    sums = [(in_hA if q < 2 else take)(PC + PX) for q in range(PIECES)]
    filler = chain(modulation("ada1", silu_c[0], "ada_b1", mods[1], sums, False),
                   modulation("mod2", silu_c[1], "mod_b2", mods[2], sums, True))
    def attend(unit):
        j, half, n = unit // 4, unit // 2 % 2, unit % 2
        hp = slice(64 * half, 64 * half + 64)
        u = unit % 2
        st = stat[:, unit, :]
        b = bank.next()
        t = PE.done(mm(psum[b], qT[hp, j, n * P:(n + 1) * P], kT[hp, :]))
        DVE.after(t)
        t = DVE.done(DVE.eng.reduce_max(st[:, 0:1], psum[b], AX.X))
        DVE.after(t)
        t = DVE.done(DVE.eng.tensor_scalar(st[:, 0:1], st[:, 0:1], -scale, None, MUL))
        SC.after(t, t_pT[u])
        t = bank.free[b] = SC.done(SC.eng.activation(prob[u], psum[b], ACT.Exp, bias=st[:, 0:1], scale=scale,
                                                     accum_out=st[:, 1:2]))
        next(filler, None)
        yield
        next(filler, None)
        DVE.after(t)
        t = DVE.done(DVE.eng.reciprocal(st[:, 2:3], st[:, 1:2]))
        DVE.after(t)
        t = DVE.done(DVE.eng.tensor_scalar(prob[u], prob[u], st[:, 2:3], None, MUL))
        PE.after(t)
        b = bank.next()
        for i in range(NT):
            ins = nc.tensor.transpose(psum[b][:, i * P:(i + 1) * P], prob[u][:, i * P:(i + 1) * P], ident)
        t = t_pT[u] = PE.done(ins)
        next(filler, None)
        yield
        next(filler, None)
        DVE.after(t, t_pv[u])
        t = bank.free[b] = DVE.done(DVE.eng.tensor_copy(probT[u], psum[b]))
        PE.after(t)
        b = bank.next()
        t = t_pv[u] = PE.done(product(psum[b][hp, 0:P], [(v[:, i, hp], probT[u][:, i * P:(i + 1) * P])
                                                         for i in range(NT)]))
        SC.after(t)
        bank.free[b] = SC.done(SC.eng.copy(feats[hp, j, n * P:(n + 1) * P], psum[b][hp, 0:P]))

    staggered(attend(unit) for unit in range(16))
    for _ in filler:
        pass
    bank.among = range(8)
    phase()
    take.at = mark1

    in_hA = Carve(hA_buf, KB * TT)
    xc = in_hA(6 * TT).rearrange("p (b t) -> p b t", b=6)
    for j in range(6):
        g0 = 1 if j == 5 else 0
        acc = xc[:, j, :].rearrange("p (g t) -> p g t", g=2)[:, g0:2, :]
        cw = cst("conv_w")[:, 3 * j:3 * j + 3]
        DVE.after(t_xp)
        t = DVE.done(DVE.eng.tensor_scalar(acc, xp[:, j, g0:2, 0:T], cw[:, 0:1], None, MUL))
        for tap in (1, 2):
            DVE.after(t)
            t = DVE.done(DVE.eng.scalar_tensor_tensor(acc, xp[:, j, g0:2, tap:tap + T], cw[:, tap:tap + 1], acc,
                                                      MUL, ADD))
        SC.after(t)
        t_xc = SC.done(SC.eng.activation(acc, acc, ACT.Silu, bias=cst("conv_b")[:, j:j + 1]))
    xs = take(NT * 512).rearrange("p (n c) -> p n c", n=NT)
    Bn = take(NT * P).rearrange("p (n c) -> p n c", n=NT)
    PE.after(t_xc)
    for n in range(NT):
        b = bank.next()
        for j in range(4):
            ins = nc.tensor.transpose(psum[b][:, j * P:(j + 1) * P], xc[:, j, n * P:(n + 1) * P], ident)
        t = PE.done(ins)
        DVE.after(t)
        t_xs = bank.free[b] = DVE.done(DVE.eng.tensor_copy(xs[:, n, :], psum[b]))
    b = bank.next()
    for n in range(NT):
        ins = nc.tensor.transpose(psum[b][:, n * P:(n + 1) * P], xc[:, 4, n * P:(n + 1) * P], ident)
    t = PE.done(ins)
    DVE.after(t)
    t_Bn = bank.free[b] = DVE.done(DVE.eng.tensor_copy(Bn, psum[b]))

    def softplus(val, n, *toks):
        mark = tiny.at
        u, z, z2, p = (tiny(n) for _ in range(4))
        SC.after(*toks)
        t = SC.done(SC.eng.activation(u, val, ACT.Abs))
        SC.after(t)
        t = SC.done(SC.eng.activation(u, u, ACT.Exp, scale=-1.0))

        def step(tok, f):
            DVE.after(tok)
            return DVE.done(f(DVE.eng))
        t = step(t, lambda e: e.tensor_scalar(z, u, 2.0, None, ADD))
        t = step(t, lambda e: e.reciprocal(z, z))
        t = step(t, lambda e: e.tensor_tensor(z, z, u, MUL))
        t = step(t, lambda e: e.tensor_tensor(z2, z, z, MUL))
        t = step(t, lambda e: e.tensor_scalar(p, z2, 2.0 / 17, None, MUL))
        for k in (15, 13, 11, 9, 7, 5, 3):
            t = step(t, lambda e: e.scalar_tensor_tensor(p, p, 2.0 / k, z2, ADD, MUL))
        t = step(t, lambda e: e.scalar_tensor_tensor(p, p, 2.0, z, ADD, MUL))
        t = step(t, lambda e: e.scalar_tensor_tensor(val, val, 0.0, p, ALU.max, ADD))
        tiny.at = mark
        return t

    dtA, wend, etot = (take(NT * 16) for _ in range(3))
    na = tiny(16)
    t = softplus(dt, NT * 16, t_dt)
    t1 = SC.done(SC.eng.activation(na, cst("a_log"), ACT.Exp))
    DVE.after(t1, t)
    v3 = lambda a: a.rearrange("p (n c) -> p n c", n=NT)
    t_dtA = t = DVE.done(DVE.eng.scalar_tensor_tensor(v3(dtA), v3(dt), -1.0, rep(na, NT), MUL, MUL))
    PE.after(t)
    b = bank.next()
    for i, lhs in enumerate((after_[0], after_[1], ones)):
        ins = mm(psum[b][:, i * 64:(i + 1) * 64], lhs, dtA)
    t = PE.done(ins)
    SC.after(t)
    for d in range(2):
        SC.done(SC.eng.activation(v3(wend)[:, :, 8 * d:8 * d + 8],
                                  v3(psum[b][:, d * 64:(d + 1) * 64])[:, :, 8 * d:8 * d + 8], ACT.Exp))
    t = bank.free[b] = SC.done(SC.eng.activation(etot, psum[b][:, 128:192], ACT.Exp))
    DVE.after(t)
    t_wend = DVE.done(DVE.eng.tensor_tensor(wend, wend, dt, MUL))

    order = ((0, 1, 2, 3), (1, 0, 3, 2))
    H = [[in_hA(256).rearrange("p (e c) -> p e c", e=4) for _ in range(2)] for _ in range(2)]
    xw = [take(512).rearrange("p (h c) -> p h c", h=8) for _ in range(2)]
    t_H = [[None, None], [None, None]]
    t_use = [None, None]
    t_last = [None, None]
    for i in range(3):
        for d in range(2):
            n = order[d][i]
            DVE.after(t_wend, t_xs, t_use[d])
            t = DVE.done(DVE.eng.tensor_tensor(xw[d], xs[:, n, :].rearrange("p (h c) -> p h c", h=8),
                                               bc(v3(wend)[:, n, 8 * d:8 * d + 8], 64), MUL))
            PE.after(t, t_Bn)
            b = bank.next()
            t = t_use[d] = PE.done(mm(psum[b], Bn[:, n, :], xw[d].rearrange("p h c -> p (h c)")))
            src, dst = H[d][max(i - 1, 0) if i < 2 else 0], H[d][0 if i < 2 else 1]
            for g in range(2):
                pp = slice(64 * g, 64 * g + 64)
                new = psum[b][pp, g * 256:(g + 1) * 256].rearrange("p (e c) -> p e c", e=4)
                DVE.after(t)
                if i == 0:
                    t1 = DVE.done(DVE.eng.tensor_copy(dst[pp], new))
                else:
                    DVE.after(t_last[d])
                    t1 = DVE.done(DVE.eng.tensor_tensor(dst[pp], src[pp],
                                                        bc(v3(etot)[pp, n, 8 * d + 4 * g:8 * d + 4 * g + 4], 64), MUL))
                    DVE.after(t1)
                    t1 = DVE.done(DVE.eng.tensor_tensor(dst[pp], dst[pp], new, ADD))
            bank.free[b] = t1
            t_last[d] = t1
    t_H = DVE.last()

    phase()
    in_xp, in_qkv = Carve(xp_buf, 6 * 2 * 258), Carve(qkv_buf, 4 * T + TT + NT * P)
    y = in_xp(4 * T).rearrange("p (j t) -> p j t", j=4)
    xdt = [in_xp(512).rearrange("p (h c) -> p h c", h=8) for _ in range(2)]
    L = [in_qkv(1024).rearrange("p (h c) -> p h c", h=8) for _ in range(2)]
    M = [take(1024).rearrange("p (h c) -> p h c", h=8) for _ in range(2)]
    CE = [in_xp(512).rearrange("p (e c) -> p e c", e=4) for _ in range(2)]
    G = [xw[d].rearrange("p h c -> p (h c)").rearrange("p (e g c) -> p e g c", e=4, g=2) for d in range(2)]
    CB = [tiny(256).rearrange("p (g c) -> p g c", g=2) for _ in range(2)]
    t_y = None
    for n in (2, 3):
        cols = slice(n * P, (n + 1) * P)
        ready = []
        for d in range(2):
            dA = v3(dtA)[:, n, 8 * d:8 * d + 8]
            DVE.after(t_dtA, t_y)
            t = DVE.done(DVE.eng.tensor_tensor(xdt[d], xs[:, n, :].rearrange("p (h c) -> p h c", h=8),
                                               bc(v3(dt)[:, n, 8 * d:8 * d + 8], 64), MUL))
            t_L = DVE.done(DVE.eng.tensor_tensor(L[d], rep(after_[d], 8), bc(dA, P), MUL))
            for g in range(2):
                t_G = DVE.done(DVE.eng.tensor_copy(G[d][:, :, g, :], bc(dA[:, 4 * g:4 * g + 4], 64)))
            PE.after(t_L, t_G)
            for half in range(2):
                b = bank.next()
                for h in range(4):
                    ins = mm(psum[b][:, h * P:(h + 1) * P], L[d][:, 4 * half + h, :], tri[d])
                t = PE.done(ins)
                SC.after(t, t_y)
                t_M = bank.free[b] = SC.done(SC.eng.activation(
                    M[d][:, 4 * half:4 * half + 4, :].rearrange("p h c -> p (h c)"), psum[b], ACT.Exp))
            for g in range(2):
                pp = slice(64 * g, 64 * g + 64)
                b = bank.next()
                t = PE.done(mm(psum[b][:, 0:P], xc[pp, 4, cols], xc[pp, 5, cols]))
                DVE.after(t)
                t = bank.free[b] = DVE.done(DVE.eng.tensor_tensor(CB[d][:, g, :], psum[b][:, 0:P], tri[d], MUL))
            DVE.after(t, t_M)
            for g in range(2):
                t_M = DVE.done(DVE.eng.tensor_tensor(M[d][:, 4 * g:4 * g + 4, :], M[d][:, 4 * g:4 * g + 4, :],
                                                     rep(CB[d][:, g, :], 4), MUL))
            b = bank.next()
            for e in range(4):
                ins = mm(psum[b][:, e * P:(e + 1) * P], G[d][:, e, :, :].rearrange("p g c -> p (g c)"), tri[d])
            t = PE.done(ins)
            SC.after(t, t_y)
            t = bank.free[b] = SC.done(SC.eng.activation(CE[d].rearrange("p e c -> p (e c)"), psum[b], ACT.Exp))
            DVE.after(t)
            t = DVE.done(DVE.eng.tensor_tensor(CE[d], CE[d], rep(xc[:, 5, cols], 4), MUL))
            ready += [t_M, t]
        PE.after(t_H, *ready)
        yb = [bank.next(), bank.next()]
        for h in range(8):
            g, e, pp = h // 4, h % 4, slice(64 * (h // 4), 64 * (h // 4) + 64)
            pairs = []
            for d in range(2):
                pairs += [(xdt[d][:, h, :], M[d][:, h, :]),
                          (H[d][order[d].index(n) - 2][pp, e, :], CE[d][pp, e, :])]
            ins = product(psum[yb[g]][64 * (h % 2):64 * (h % 2) + 64, (e // 2) * P:(e // 2 + 1) * P], pairs)
        t = t_y = PE.done(ins)
        DVE.after(t)
        for j in range(4):
            t = DVE.done(DVE.eng.scalar_tensor_tensor(y[:, j, cols.start - T:cols.stop - T], xc[:, j, cols],
                                                      cst("d_skip")[:, j:j + 1],
                                                      psum[yb[j // 2]][:, (j % 2) * P:(j % 2 + 1) * P],
                                                      MUL, ADD))
        bank.free[yb[0]] = bank.free[yb[1]] = t
    DVE.after(t)
    t = DVE.done(DVE.eng.tensor_tensor(y, y, zs, MUL))
    phase()
    in_qkv = Carve(qkv_buf, 4 * T + TT + NT * P)
    sq = in_qkv(4 * T).rearrange("p (j t) -> p j t", j=4)
    rs = in_qkv(2 * T).rearrange("p (g t) -> p g t", g=2)
    for g in range(2):
        t1 = rstd_of(y[:, 2 * g:2 * g + 2, :], 2, T, 256, rs[:, g, :], sq[:, 2 * g:2 * g + 2, :], t)
        DVE.after(t1)
        for j in (2 * g, 2 * g + 1):
            t2 = DVE.done(DVE.eng.scalar_tensor_tensor(feats[:, 4 + j, :], y[:, j, :], cst("ssm_norm")[:, j:j + 1],
                                                       rs[:, g, :], MUL, MUL))
    residual(feats, lambda j: (START["hyo"] + j // TB, (j % TB) * P), 2, t2)
    phase()

    take.at = 0
    h = take(KB * T).rearrange("p (k t) -> p k t", k=KB)
    normed(x, h, "norm_ffn0", 3, 4, 0, DVE.last())
    ffn("ffn0", h, NFFN, 5, SLOTS)

    mod = mods[1]
    normed(x, h, "norm_mix1", 0, 1, 0, DVE.last())
    phase()
    mark1 = take.at
    cu = take(KB * 258).rearrange("p (k t) -> p k t", k=KB)
    gb = take(KB * T).rearrange("p (k t) -> p k t", k=KB)
    gc = take(KB * T).rearrange("p (k t) -> p k t", k=KB)
    t_pad = GP.done(GP.eng.memset(cu, 0.0))
    sc = START["sc"]
    for i in range(4):
        arrive(sc + i)
        for jj in range(2):
            j = 2 * i + jj
            banks = [bank.next() for _ in range(3)]
            for part in range(3):
                c = (3 * jj + part) * P
                ins = product(psum[banks[part]][:, 0:T], [(proj(sc + i)[:, k, c:c + P], h[:, k, :]) for k in range(KB)])
            t = PE.done(ins)
            SC.after(t)
            bank.free[banks[0]] = SC.done(SC.eng.copy(gb[:, j, :], psum[banks[0]][:, 0:T]))
            t1 = bank.free[banks[1]] = SC.done(SC.eng.copy(gc[:, j, :], psum[banks[1]][:, 0:T]))
            DVE.after(t1, t_pad)
            t = bank.free[banks[2]] = DVE.done(DVE.eng.tensor_tensor(cu[:, j, 1:T + 1], gc[:, j, :],
                                                                     psum[banks[2]][:, 0:T], MUL))
            DVE.after(t)
            cw = cst("sc_conv")[:, 3 * j:3 * j + 3]
            t = DVE.done(DVE.eng.tensor_scalar(gc[:, j, :], cu[:, j, 0:T], cw[:, 0:1], None, MUL))
            for tap in (1, 2):
                DVE.after(t)
                t = DVE.done(DVE.eng.scalar_tensor_tensor(gc[:, j, :], cu[:, j, tap:tap + T], cw[:, tap:tap + 1],
                                                          gc[:, j, :], MUL, ADD))
            DVE.after(t)
            t = DVE.done(DVE.eng.tensor_tensor(gb[:, j, :], gb[:, j, :], gc[:, j, :], MUL))
        free_tile(sc + i)
    residual(gb, lambda j: (sc + 4, j * P) if j < TB else (sc + 5, (j - TB) * P), 2, t)
    phase()
    take.at = mark1
    normed(x, h, "norm_ffn1", 3, 4, 0, DVE.last())
    ffn("ffn1", h, NFFN, 5, SLOTS)
    normed(x, x, "final1", None, None, 0, DVE.last())
    phase()

    phase()
    bank.free = [None] * 8
    take.at = 0
    mod = mods[2]
    t_mod = DVE.last()
    feats = take(KB * T).rearrange("p (k t) -> p k t", k=KB)
    mark_feats = take.at
    hA_buf = take(KB * TT)
    hA = hA_buf.rearrange("p (k t) -> p k t", k=KB)
    mark0 = take.at
    cx = take(KB * T).rearrange("p (k t) -> p k t", k=KB)
    nc.gpsimd.dma_start(cx, ctx2).then_inc(ctx_in, 16)
    tc_ = normed(cx, hA[:, :, 0:T], "norm1_2", 0, 1, 1, t_mod, (ctx_in, 32, "ctx_in"))
    normed(x, hA[:, :, T:TT], "norm1_2", 0, 1, 0, *tc_)
    phase()
    take.at = mark0
    in2 = START["in2"]
    ba = tiny(NT * 16)
    ba3 = v3(ba)
    b = bank.next()
    for n in range(NT):
        ins = product(psum[b][:, n * 16:(n + 1) * 16],
                      [(hA[:, k, n * P:(n + 1) * P], cst("w_ba")[:, k * 16:(k + 1) * 16]) for k in range(KB)])
    t = PE.done(ins)
    DVE.after(t)
    t_ba = bank.free[b] = DVE.done(DVE.eng.tensor_copy(ba, psum[b][:, 0:64]))

    HH = 4
    zs2 = take(4 * T).rearrange("p (j t) -> p j t", j=4)
    qh = take(4 * T).rearrange("p (j t) -> p j t", j=4)
    vh = take(2 * 512).rearrange("p (n c) -> p n c", n=2)
    kh = take(2 * 1024).rearrange("p (n c) -> p n c", n=2)
    lf = take(2 * 1024).rearrange("p (n c) -> p n c", n=2)
    Sh = [[take(512) for _ in range(2)] for _ in range(2)]
    E = [take(1024).rearrange("p (l t) -> p l t", l=8) for _ in range(2)]
    kT2 = take(2 * P).rearrange("p (d t) -> p d t", d=2)
    ksum = take(P)
    att = take(P)
    kd = [E[d].rearrange("p l t -> p (l t)")[:, 0:512] for d in range(2)]
    eth = [tiny(4) for _ in range(2)]

    def gates_natural(tok0):
        for c in range(6):
            tile, cc = in2 + c // 3, (c % 3) * 256
            if tok0 == 0 and c % 3 == 0:
                arrive(tile)
            b = bank.next()
            for n in range(2):
                ins = product(psum[b][:, n * 256:(n + 1) * 256],
                              [(hA[:, k, (tok0 + n) * P:(tok0 + n + 1) * P], proj(tile)[:, k, cc:cc + 256])
                               for k in range(KB)])
            t = PE.done(ins)
            raw = psum[b].rearrange("p (n c) -> p n c", n=2)
            if c < 2:
                SC.after(t)
                bank.free[b] = SC.done(SC.eng.copy(vh[:, :, c * 256:(c + 1) * 256], raw))
                continue
            l, k_ = lf[:, :, (c - 2) * 256:(c - 1) * 256], kh[:, :, (c - 2) * 256:(c - 1) * 256]
            SC.after(t)
            t1 = SC.done(SC.eng.activation(l, raw, ACT.Abs))
            SC.after(t1)
            t1 = SC.done(SC.eng.activation(l, l, ACT.Exp, scale=-1.0))
            SC.after(t1)
            t1 = SC.done(SC.eng.activation(k_, l, ACT.Ln, bias=1.0))
            DVE.after(t1)
            t1 = DVE.done(DVE.eng.tensor_scalar(l, raw, 0.0, None, ALU.min))
            DVE.after(t1)
            t1 = DVE.done(DVE.eng.tensor_tensor(l, l, k_, SUB))
            DVE.after(t1)
            t1 = bank.free[b] = DVE.done(DVE.eng.tensor_tensor(k_, l, raw, SUB))
            SC.after(t1)
            SC.done(SC.eng.activation(k_, k_, ACT.Exp))
        return SC.last(), DVE.last()

    def hg_state(d, n, src, dst, *toks):
        f = lf[:, n, d * 512:(d + 1) * 512]
        b = bank.next()
        PE.after(*toks)
        t = PE.done(mm(psum[b], after_[d], f))
        SC.after(t)
        t = bank.free[b] = SC.done(SC.eng.activation(kd[d], psum[b], ACT.Exp))
        DVE.after(t)
        t_kd = DVE.done(DVE.eng.tensor_tensor(kd[d], kd[d], kh[:, n, d * 512:(d + 1) * 512], MUL))
        b = bank.next()
        for h in range(HH):
            ins = mm(psum[b][:, h:h + 1], f[:, h * P:(h + 1) * P], ones[:, 0:1])
        t = PE.done(ins)
        SC.after(t)
        t_e = bank.free[b] = SC.done(SC.eng.activation(eth[d], psum[b][:, 0:4], ACT.Exp))
        PE.after(t_kd)
        b = bank.next()
        for h in range(HH):
            ins = mm(psum[b][:, h * P:(h + 1) * P], kd[d][:, h * P:(h + 1) * P], vh[:, n, h * P:(h + 1) * P])
        t = PE.done(ins)
        DVE.after(t, t_e)
        if src is None:
            t = DVE.done(DVE.eng.tensor_copy(dst, psum[b]))
        else:
            h4 = lambda a: a.rearrange("p (h e) -> p h e", h=HH)
            t = DVE.done(DVE.eng.tensor_tensor(h4(dst), h4(src), bc(eth[d], P), MUL))
            DVE.after(t)
            t = DVE.done(DVE.eng.tensor_tensor(dst, dst, psum[b], ADD))
        bank.free[b] = t
        return t

    toks = gates_natural(0)
    for i in range(2):
        for d in range(2):
            hg_state(d, order[d][i], None if i == 0 else Sh[d][0], Sh[d][0], *toks, DVE.last(), SC.last())
    phase()
    toks = gates_natural(2)
    free_tile(in2, in2 + 1)
    for part in range(2):
        arrive(in2 + 2 + part)
        for j in range(TB):
            o = part * TB + j
            b = bank.next()
            t = PE.done(product(psum[b][:, 0:T], block_rows(in2 + 2 + part, j * P, T, TT)))
            SC.after(t)
            dst = (qh, feats[:, 0:4, :], zs2)[o // 4][:, o % 4, :]
            bank.free[b] = SC.done(SC.eng.activation(dst, psum[b][:, 0:T], ACT.Silu))
        free_tile(in2 + 2 + part)
    t_q = SC.last()
    gsil = feats[:, 0:4, :]
    for d in range(2):
        t = hg_state(d, order[d][2] - 2, Sh[d][0], Sh[d][1], *toks, DVE.last())
    phase()

    mask = (cst("maskF"), cst("maskB"))
    spans = (cst("spanF"), cst("spanB"))
    t_free = [None, None]
    second = [take(1024).rearrange("p (l t) -> p l t", l=8) for _ in range(2)]
    Es = [E, second]
    kTs = [kT2, take(2 * P).rearrange("p (d t) -> p d t", d=2)]
    ksums, atts = [ksum, take(P)], [att, take(P)]

    def hg_unit(unit):
        n, h, u = unit // HH, unit % HH, unit % 2
        cols = slice(n * P, (n + 1) * P)
        E, kT2, ksum, att = Es[u], kTs[u], ksums[u], atts[u]
        q = qh[:, h, cols]
        b = bank.next()
        for d in range(2):
            ins = nc.tensor.transpose(psum[b][:, d * P:(d + 1) * P], kh[:, n, d * 512 + h * P:d * 512 + (h + 1) * P],
                                      ident)
        t = PE.done(ins)
        DVE.after(t, t_free[u])
        t_kT = bank.free[b] = DVE.done(DVE.eng.tensor_copy(kT2.rearrange("p d t -> p (d t)"), psum[b][:, 0:256]))
        DVE.after(t_kT)
        t_ks = DVE.done(DVE.eng.tensor_tensor(ksum, kT2[:, 0, :], kT2[:, 1, :], ADD))
        t_E = []
        for d in range(2):
            f = lf[:, n, d * 512 + h * P:d * 512 + (h + 1) * P]
            Ef = E[d].rearrange("p l t -> p (l t)")
            for half in range(2):
                b = bank.next()
                t = PE.done(mm(psum[b], f, spans[d][:, half * 512:(half + 1) * 512]))
                SC.after(t, t_free[u])
                bank.free[b] = SC.done(SC.eng.activation(Ef[:, half * 512:(half + 1) * 512], psum[b], ACT.Exp))
            t_E.append(bank.free[b])
        yield
        b = bank.next()
        PE.after(t_ks)
        t = PE.done(mm(psum[b][:, 0:P], ksum, q))
        DVE.after(t)
        t_att = bank.free[b] = DVE.done(DVE.eng.tensor_tensor(att, psum[b][:, 0:P], ident, MUL))
        for d in range(2):
            DVE.after(t_E[d], t_kT)
            GP.after(t_E[d], t_kT)
            for li, lev in enumerate(LEVELS):
                Ev = E[d][:, li, :].rearrange("p (m s c) -> p m s c", s=2, c=lev)
                qv = q.rearrange("p (m s c) -> p m s c", s=2, c=lev)
                kv = kT2[:, d, :].rearrange("p (m s c) -> p m s c", s=2, c=lev)
                tq, ts = (1, 0) if d == 0 else (0, 1)
                t1 = DVE.done(DVE.eng.tensor_tensor(Ev[:, :, tq, :], Ev[:, :, tq, :], qv[:, :, tq, :], MUL))
                t2 = GP.done(GP.eng.tensor_tensor(Ev[:, :, ts, :], Ev[:, :, ts, :], kv[:, :, ts, :], MUL))
            t_qd = DVE.done(DVE.eng.tensor_tensor(E[d][:, 7, :], E[d][:, 7, :], q, MUL))
            if d == 0:
                yield
            PE.after(t1, t2, t_qd)
            for l0, l1 in ((0, 4), (4, 7)):
                b = bank.next()
                for li in range(l0, l1):
                    ins = mm(psum[b][:, (li - l0) * P:(li - l0 + 1) * P], E[d][:, li, :], E[d][:, li, :])
                t = PE.done(ins)
                for li in range(l0, l1):
                    DVE.after(t, t_att)
                    t_att = DVE.done(DVE.eng.copy_predicated(att, mask[d][:, li * P:(li + 1) * P].bitcast(U32),
                                                             psum[b][:, (li - l0) * P:(li - l0 + 1) * P]))
                bank.free[b] = t_att
            yield
        PE.after(t_att, t_q)
        b = bank.next()
        hs = slice(h * P, (h + 1) * P)
        t = t_free[u] = PE.done(product(psum[b][:, 0:P],
                                        [(vh[:, n, hs], att),
                                         (Sh[0][n][:, hs], E[0][:, 7, :]), (Sh[1][1 - n][:, hs], E[1][:, 7, :])]))
        SC.after(t)
        bank.free[b] = SC.done(SC.eng.copy(q, psum[b][:, 0:P]))

    staggered(hg_unit(unit) for unit in range(2 * HH))

    def head_gate(o, gate, weight, out_):
        phase()
        mark = take.at
        sq = take(4 * T).rearrange("p (j t) -> p j t", j=4)
        rs = take(4 * T).rearrange("p (j t) -> p j t", j=4)
        t = SC.done(SC.eng.activation(sq, o, ACT.Square))
        for g in range(2):
            b = bank.next()
            PE.after(t)
            t1 = PE.done(mm(psum[b], ones, sq[:, 2 * g:2 * g + 2, :].rearrange("p j t -> p (j t)")))
            SC.after(t1)
            t2 = bank.free[b] = SC.done(SC.eng.activation(rs[:, 2 * g:2 * g + 2, :].rearrange("p j t -> p (j t)"),
                                                          psum[b], ACT.Sqrt, bias=eps, scale=1.0 / P))
        DVE.after(t2)
        t = DVE.done(DVE.eng.reciprocal(rs, rs))
        DVE.after(t)
        fl = lambda a: a.rearrange("p j t -> p (j t)")
        t = DVE.done(DVE.eng.scalar_tensor_tensor(fl(rs), fl(o), cst(weight), fl(rs), MUL, MUL))
        DVE.after(t)
        t = DVE.done(DVE.eng.tensor_tensor(out_, rs, gate, MUL))
        phase()
        take.at = mark

    phase()
    in_hg = Carve(lf.rearrange("p n c -> p (n c)"), 2048)
    saved_take, take = take, in_hg
    head_gate(qh, gsil, "hg_norm", feats[:, 0:4, :])
    take = saved_take

    take.at = mark0 + 4 * T
    dq = take(4 * T).rearrange("p (j t) -> p j t", j=4)
    dk = take(4 * TT).rearrange("p (j t) -> p j t", j=4)
    kn = take(NT * 512).rearrange("p (n c) -> p n c", n=NT)
    vn = take(NT * 512).rearrange("p (n c) -> p n c", n=NT)
    GW = 64
    GR = T // GW
    pads = [take((GR + 2) * (GW + 2) + T + 2) for _ in range(2)]
    dvt = [take(TT) for _ in range(2)]
    for p_ in pads:
        t_pad = GP.done(GP.eng.memset(p_, 0.0))
    t_used = [None, None]
    t_tr = [None, None]
    def turn_v(o, t):
        PE.after(t)
        b = bank.next()
        for n in range(NT):
            ins = nc.tensor.transpose(psum[b][:, n * P:(n + 1) * P], dvt[o % 2][:, n * P:(n + 1) * P], ident)
        t = t_tr[o % 2] = PE.done(ins)
        SC.after(t)
        bank.free[b] = SC.done(SC.eng.copy(vn[:, :, (o % 4) * P:(o % 4 + 1) * P],
                                           psum[b].rearrange("p (n c) -> p n c", n=NT)))

    for o in range(12):
        tile = in2 + 4 + o // TB
        if o % TB == 0:
            arrive(tile)
        j, u = o % 4, o % 2
        n0 = T if o < 4 else 0
        b = bank.next()
        t = PE.done(product(psum[b][:, n0:TT], block_rows(tile, (o % TB) * P, n0, TT)))
        if o % TB == TB - 1:
            free_tile(tile)
        if o >= 9:
            turn_v(o - 1, t_conv)
        grid = pads[u][:, 0:(GR + 2) * (GW + 2)].rearrange("p (r c) -> p r c", r=GR + 2)
        line = pads[u][:, (GR + 2) * (GW + 2):]
        SC.after(t, t_used[u], t_pad)
        t = SC.done(SC.eng.copy(grid[:, 1:GR + 1, 1:GW + 1], psum[b][:, T:TT].rearrange("p (r c) -> p r c", r=GR)))
        if o >= 4:
            t = SC.done(SC.eng.copy(line[:, 1:T + 1], psum[b][:, 0:T]))
        bank.free[b] = t
        dst = dq[:, j, :] if o < 4 else dk[:, j, :] if o < 8 else dvt[u]
        lat = (dst if o < 4 else dst[:, T:TT])
        lat3 = lat.rearrange("p (r c) -> p r c", r=GR)
        cw = cst("dn_conv")[:, 9 * o:9 * o + 9]
        DVE.after(t, t_tr[u])
        for tap in range(9):
            src = grid[:, tap // 3:tap // 3 + GR, tap % 3:tap % 3 + GW]
            if tap == 0:
                t = DVE.done(DVE.eng.tensor_scalar(lat3, src, cw[:, 0:1], None, MUL))
            else:
                t = DVE.done(DVE.eng.scalar_tensor_tensor(lat3, src, cw[:, tap:tap + 1], lat3, MUL, ADD))
            DVE.after(t)
        if o >= 4:
            for tap in range(3):
                src = line[:, tap:tap + T]
                if tap == 0:
                    t = DVE.done(DVE.eng.tensor_scalar(dst[:, 0:T], src, cw[:, 3:4], None, MUL))
                else:
                    t = DVE.done(DVE.eng.scalar_tensor_tensor(dst[:, 0:T], src, cw[:, 3 + tap:4 + tap], dst[:, 0:T],
                                                              MUL, ADD))
                DVE.after(t)
        t_used[u] = t
        SC.after(t)
        t = SC.done(SC.eng.activation(dst, dst, ACT.Silu))
        t_conv = t
    turn_v(11, t_conv)
    phase()
    in_hA = Carve(hA_buf, KB * TT)
    sq2, rsn2 = [in_hA(512) for _ in range(2)], [in_hA(512) for _ in range(2)]
    t_sq, t_rs = [None, None], [None, None]
    for i in range(6):
        src = (dq[:, 2 * i:2 * i + 2, :] if i < 2 else dk[:, i - 2:i - 1, :]).rearrange("p j t -> p (j t)")
        sq, rsn, u = sq2[i % 2], rsn2[i % 2], i % 2
        SC.after(t_sq[u], t_rs[u])
        t = SC.done(SC.eng.activation(sq, src, ACT.Square))
        PE.after(t)
        b = bank.next()
        t = t_sq[u] = PE.done(mm(psum[b], ones, sq))
        SC.after(t)
        t = bank.free[b] = SC.done(SC.eng.activation(rsn, psum[b], ACT.Sqrt, bias=eps))
        DVE.after(t)
        t = DVE.done(DVE.eng.reciprocal(rsn, rsn))
        DVE.after(t)
        t = t_rs[u] = DVE.done(DVE.eng.scalar_tensor_tensor(src, src, P ** -0.5 if i < 2 else 1.0, rsn, MUL, MUL))
    PE.after(t)
    for n in range(NT):
        b = bank.next()
        for h in range(HH):
            ins = nc.tensor.transpose(psum[b][:, h * P:(h + 1) * P], dk[:, h, n * P:(n + 1) * P], ident)
        t = PE.done(ins)
        SC.after(t)
        bank.free[b] = SC.done(SC.eng.copy(kn[:, n, :], psum[b]))

    beta, la, ecum, ekd, etd = (tiny(NT * 8) for _ in range(5))
    b8 = lambda a: a.rearrange("p (n c) -> p n c", n=NT)
    SC.after(t_ba)
    t = SC.done(SC.eng.activation(b8(beta), ba3[:, :, 0:8], ACT.Exp, scale=-1.0))
    DVE.after(t)
    t = DVE.done(DVE.eng.tensor_scalar(beta, beta, 1.0, None, ADD))
    DVE.after(t)
    t = DVE.done(DVE.eng.reciprocal(beta, beta))
    t = DVE.done(DVE.eng.tensor_tensor(b8(la), ba3[:, :, 8:16], rep(cst("dn_dtb"), NT), ADD))
    t = softplus(la, NT * 8, t)
    na8 = tiny(8)
    SC.after(t)
    t1 = SC.done(SC.eng.activation(na8, cst("dn_alog"), ACT.Exp))
    DVE.after(t, t1)
    t = DVE.done(DVE.eng.scalar_tensor_tensor(b8(la), b8(la), -1.0, rep(na8, NT), MUL, MUL))
    PE.after(t)
    b = bank.next()
    for i, lhs in enumerate((tri[0], tri[1], after_[0], after_[1], ones)):
        ins = mm(psum[b][:, i * 32:(i + 1) * 32], lhs, la)
    t = PE.done(ins)
    SC.after(t)
    for d in range(2):
        hd = slice(4 * d, 4 * d + 4)
        SC.done(SC.eng.activation(b8(ecum)[:, :, hd], b8(psum[b][:, d * 32:(d + 1) * 32])[:, :, hd], ACT.Exp))
        SC.done(SC.eng.activation(b8(ekd)[:, :, hd], b8(psum[b][:, (2 + d) * 32:(3 + d) * 32])[:, :, hd], ACT.Exp))
    bank.free[b] = SC.done(SC.eng.activation(etd, psum[b][:, 128:160], ACT.Exp))
    phase()

    in_hA = Carve(hA_buf, KB * TT)
    assert pads[0].shape[1] >= 512 and TT >= 512
    sets = [[[(in_hA if st == 0 else take)(512) for _ in range(4)] + [take(512)] for _ in range(2)] for st in range(2)]
    S = [take(512) for _ in range(2)]
    RH = [p_[:, 0:512] for p_ in pads]
    kdc = [d_[:, 0:512] for d_ in dvt]
    h4 = lambda a: a.rearrange("p (h c) -> p h c", h=HH)
    od = feats[:, 4:8, :]
    strict = (after_[1], after_[0])

    def heads_mm(b, f, *toks):
        PE.after(*toks)
        for h in range(HH):
            a, c = f(h)
            ins = mm(psum[b][:, h * P:(h + 1) * P], a, c)
        return PE.done(ins)

    def prepare(step, d):
        NT_, Tm, TTm, Z, Dm = sets[step % 2][d]
        n = order[d][step]
        cols = slice(n * P, (n + 1) * P)
        dl = b8(la)[:, n, 4 * d:4 * d + 4]
        db = b8(beta)[:, n, 4 * d:4 * d + 4]
        t_L = DVE.done(DVE.eng.tensor_tensor(h4(Z), rep(after_[d], HH), bc(dl, P), MUL))
        b = bank.next()
        t_b = heads_mm(b, lambda h: (db[:, h:h + 1].broadcast_to([P, P]), ident))
        DVE.after(t_b)
        t_kb = bank.free[b] = DVE.done(DVE.eng.tensor_tensor(h4(Tm), h4(psum[b]), dk[:, :, cols], MUL))
        b = bank.next()
        t = heads_mm(b, lambda h: (h4(Z)[:, h, :], tri[d]), t_L)
        SC.after(t)
        t_D = bank.free[b] = SC.done(SC.eng.activation(Dm, psum[b], ACT.Exp))
        yield
        b = bank.next()
        t = heads_mm(b, lambda h: (dk[:, h, cols], h4(Tm)[:, h, :]), t_kb)
        DVE.after(t, t_D)
        t = bank.free[b] = DVE.done(DVE.eng.tensor_tensor(NT_, psum[b], Dm, MUL))
        DVE.after(t)
        t = DVE.done(DVE.eng.tensor_tensor(h4(NT_), h4(NT_), rep(strict[d], HH), MUL))
        yield
        DVE.after(t)
        t = DVE.done(DVE.eng.tensor_tensor(h4(Z), h4(NT_), rep(mask[d][:, 0:P], HH), MUL))
        DVE.after(t)
        t_TT = DVE.done(DVE.eng.tensor_tensor(h4(TTm), rep(ident, HH), h4(Z), SUB))
        PE.after(t)
        b = bank.next()
        for h in range(HH):
            ins = nc.tensor.transpose(psum[b][:, h * P:(h + 1) * P], h4(Z)[:, h, :], ident)
        t = PE.done(ins)
        yield
        DVE.after(t)
        ready = bank.free[b] = DVE.done(DVE.eng.tensor_tensor(h4(Tm), rep(ident, HH), h4(psum[b]), SUB))
        for li in range(1, len(LEVELS)):
            b = bank.next()
            t = heads_mm(b, lambda h: (h4(NT_)[:, h, :], h4(Tm)[:, h, :]), ready)
            DVE.after(t)
            t = bank.free[b] = DVE.done(DVE.eng.tensor_tensor(
                h4(Z), h4(psum[b]), rep(mask[1 - d][:, li * P:(li + 1) * P], HH), MUL))
            yield
            last = li == len(LEVELS) - 1
            b2 = bank.next()
            t2 = heads_mm(b2, lambda h: (h4(Z)[:, h, :], h4(TTm)[:, h, :]), t)
            if not last:
                b1 = bank.next()
                t1 = heads_mm(b1, lambda h: (h4(TTm)[:, h, :], h4(Z)[:, h, :]))
                DVE.after(t1)
                ready = bank.free[b1] = DVE.done(DVE.eng.tensor_tensor(Tm, Tm, psum[b1], SUB))
            DVE.after(t1, t2)
            ready = bank.free[b2] = DVE.done(DVE.eng.tensor_tensor(TTm, TTm, psum[b2], SUB))
            yield

    t_S = [None, None]

    def recur(step, d):
        _, Tm, TTm, vnew, Dm = sets[step % 2][d]
        n = order[d][step]
        cols = slice(n * P, (n + 1) * P)
        col = lambda a: b8(a)[:, n, 4 * d:4 * d + 4]
        if step == 0:
            t = DVE.done(DVE.eng.tensor_tensor(h4(RH[d]), h4(vn[:, n, :]), bc(col(beta), P), MUL))
        else:
            b = bank.next()
            t = heads_mm(b, lambda h: (dk[:, h, cols], h4(S[d])[:, h, :]), t_S[d])
            DVE.after(t)
            t = bank.free[b] = DVE.done(DVE.eng.tensor_tensor(h4(RH[d]), h4(psum[b]), bc(col(ecum), P), MUL))
            DVE.after(t)
            t = DVE.done(DVE.eng.tensor_tensor(RH[d], vn[:, n, :], RH[d], SUB))
            DVE.after(t)
            t = DVE.done(DVE.eng.tensor_tensor(h4(RH[d]), h4(RH[d]), bc(col(beta), P), MUL))
        t_kd = DVE.done(DVE.eng.tensor_tensor(h4(kdc[d]), h4(kn[:, n, :]), bc(col(ekd), P), MUL))
        if step >= 2:
            lat = slice(cols.start - T, cols.stop - T)
            t0 = DVE.done(DVE.eng.tensor_tensor(h4(Dm), h4(Dm), rep(tri[d], HH), MUL))
            b = bank.next()
            t1 = heads_mm(b, lambda h: (dk[:, h, cols], dq[:, h, lat]))
            DVE.after(t0, t1)
            t_qk = bank.free[b] = DVE.done(DVE.eng.tensor_tensor(Dm, Dm, psum[b], MUL))
            b = bank.next()
            t1 = heads_mm(b, lambda h: (col(la)[:, h:h + 1].broadcast_to([P, P]), tri[d]))
            SC.after(t1)
            t1 = bank.free[b] = SC.done(SC.eng.activation(Tm, psum[b], ACT.Exp))
            DVE.after(t1)
            t_qd = DVE.done(DVE.eng.tensor_tensor(h4(Tm), h4(Tm), dq[:, :, lat], MUL))
        yield
        b = bank.next()
        t = heads_mm(b, lambda h: (h4(TTm)[:, h, :], h4(RH[d])[:, h, :]), t)
        SC.after(t)
        t_v = bank.free[b] = SC.done(SC.eng.copy(vnew, psum[b]))
        yield
        if step >= 2:
            b = bank.next()
            PE.after(t_v, t_qk, t_qd)
            for h in range(HH):
                ins = product(psum[b][:, h * P:(h + 1) * P],
                              [(h4(vnew)[:, h, :], h4(Dm)[:, h, :]), (h4(S[d])[:, h, :], h4(Tm)[:, h, :])])
            t_o = PE.done(ins)
            DVE.after(t_o, t_od[n - 2])
            if t_od[n - 2] is None:
                t = DVE.done(DVE.eng.tensor_copy(od[:, :, lat], h4(psum[b])))
            else:
                t = DVE.done(DVE.eng.tensor_tensor(od[:, :, lat], od[:, :, lat], h4(psum[b]), ADD))
            t_od[n - 2] = bank.free[b] = t
        if step < 3:
            b = bank.next()
            t = heads_mm(b, lambda h: (h4(kdc[d])[:, h, :], h4(vnew)[:, h, :]), t_kd, t_v)
            DVE.after(t)
            if step == 0:
                t = DVE.done(DVE.eng.tensor_copy(S[d], psum[b]))
            else:
                t = DVE.done(DVE.eng.tensor_tensor(h4(S[d]), h4(S[d]), bc(col(etd), P), MUL))
                DVE.after(t)
                t = DVE.done(DVE.eng.tensor_tensor(S[d], S[d], psum[b], ADD))
            bank.free[b] = t_S[d] = t
        yield

    t_od = [None, None]
    for pair in ((0, 1), (2, 3)):
        phase()
        staggered((prepare(step, d) for step in pair for d in range(2)), 4)
        for step in pair:
            phase()
            staggered(recur(step, d) for d in range(2))
    phase()
    take.at = mark0 + 4 * T
    head_gate(od, zs2, "dn_norm", od)
    out2 = START["out2"]
    residual(feats, lambda j: (out2, j * P) if j < TB else (out2 + 1, (j - TB) * P), 2)
    phase()
    take.at = 0
    h = take(KB * T).rearrange("p (k t) -> p k t", k=KB)
    normed(x, h, "norm2_2", 3, 4, 0, DVE.last())
    phase()
    gbc = arena[:, 0:EXPERTS * T].rearrange("p (e t) -> p e t", e=EXPERTS)
    mark_t = tiny.at
    tiny.at = 128
    lg = tiny(40).rearrange("p (n c) -> p n c", n=2)
    b = bank.next()
    for n in range(2):
        ins = product(psum[b][:, n * 20:(n + 1) * 20],
                      [(h[:, k, n * P:(n + 1) * P], cst("w_rt")[:, k * 20:(k + 1) * 20]) for k in range(KB)])
    t = PE.done(ins)
    DVE.after(t)
    t = bank.free[b] = DVE.done(DVE.eng.tensor_tensor(lg, psum[b][:, 0:40].rearrange("p (n c) -> p n c", n=2),
                                                      rep(cst("b_rt"), 2), ADD))

    def vec(f, *toks):
        DVE.after(DVE.last(), *toks)
        return DVE.done(f(DVE.eng))

    def pick(src):
        m, eq, m2 = tiny(2), tiny(8), tiny(2)
        eq = eq.rearrange("p (n c) -> p n c", n=2)
        vec(lambda e: e.tensor_reduce(m, src, AX.X, ALU.max))
        vec(lambda e: e.tensor_tensor(eq, src, bc(m, 4), ALU.is_equal))
        vec(lambda e: e.tensor_tensor(eq, eq, rep(cst("first4"), 2), MUL))
        vec(lambda e: e.tensor_reduce(m2, eq, AX.X, ALU.max))
        vec(lambda e: e.tensor_tensor(eq, eq, bc(m2, 4), ALU.is_equal))
        return m, eq

    n4 = lambda: tiny(8).rearrange("p (n c) -> p n c", n=2)
    gl = lg[:, :, 0:4]
    gm, goh = pick(gl)
    ex, gw = n4(), tiny(2)
    t = vec(lambda e: e.tensor_tensor(ex, gl, bc(gm, 4), SUB))
    SC.after(t)
    t = SC.done(SC.eng.activation(ex, ex, ACT.Exp))
    vec(lambda e: e.tensor_reduce(gw, ex, AX.X, ADD), t)
    vec(lambda e: e.reciprocal(gw, gw))
    el, es = tiny(32).rearrange("p (n e g) -> p n e g", n=2, e=4), n4()
    for n in range(2):
        vec(lambda e: e.tensor_tensor(el[:, n], lg[:, n, 4:20].rearrange("p (g e) -> p e g", g=4),
                                      rep(goh[:, n, :], 4), MUL))
    vec(lambda e: e.tensor_reduce(es.rearrange("p n c -> p (n c)"), el.rearrange("p n e g -> p (n e) g"), AX.X, ADD))
    v1, oh1 = pick(es)
    rest = n4()
    vec(lambda e: e.scalar_tensor_tensor(rest, oh1, -1e30, es, MUL, ADD))
    v2, oh2 = pick(rest)
    e2, w1, w2_ = tiny(2), tiny(2), tiny(2)
    t = vec(lambda e: e.tensor_tensor(e2, v2, v1, SUB))
    SC.after(t)
    t = SC.done(SC.eng.activation(e2, e2, ACT.Exp))
    vec(lambda e: e.tensor_scalar(w1, e2, 1.0, None, ADD), t)
    vec(lambda e: e.reciprocal(w1, w1))
    vec(lambda e: e.tensor_tensor(w1, w1, gw, MUL))
    vec(lambda e: e.tensor_tensor(w2_, w1, e2, MUL))
    vec(lambda e: e.tensor_tensor(oh1, oh1, bc(w1, 4), MUL))
    vec(lambda e: e.tensor_tensor(oh2, oh2, bc(w2_, 4), MUL))
    vec(lambda e: e.tensor_tensor(oh1, oh1, oh2, ADD))
    gt = tiny(32).rearrange("p (n g e) -> p n g e", n=2, g=4)
    for n in range(2):
        t = vec(lambda e: e.tensor_tensor(gt[:, n], bc(goh[:, n, :], 4), rep(oh1[:, n, :], 4), MUL))

    def spread_gates(dst):
        for e_ in range(0, EXPERTS, 2):
            b = bank.next()
            for ee in range(2):
                for n in range(2):
                    g_ = gt[:, n, (e_ + ee) // 4, (e_ + ee) % 4:(e_ + ee) % 4 + 1]
                    ins = mm(psum[b][:, (2 * ee + n) * P:(2 * ee + n + 1) * P], g_.broadcast_to([P, P]), ident)
            t = PE.done(ins)
            SC.after(t, DVE.last())
            bank.free[b] = SC.done(SC.eng.copy(dst[:, e_:e_ + 2, :].rearrange("p e t -> p (e t)"), psum[b]))

    ffn("moe", h, NMOE, 5, 2 * SLOTS, gates=gbc)
    normed(x, x, "final2", None, None, 0, DVE.last())
    finish(x, out)


def _host(inputs):
    f = np.float32
    g = {k: np.asarray(a) for k, a in inputs.items()}

    def kblocks(w):
        return w.reshape(w.shape[0] // P, P, w.shape[1]).transpose(1, 0, 2)

    def tiles(w):
        return [kblocks(w[:, a:a + TC]).reshape(P, TILE) for a in range(0, w.shape[1], TC)]

    def pad(w):
        n = -w.shape[1] % TC
        return np.concatenate([w, np.zeros((w.shape[0], n), f)], 1) if n else w

    def ada(w):
        return [w[k * P:(k + 1) * P] for k in range(KB)]

    def ffn(wg, wu, wd):
        out = []
        for a in range(0, wg.shape[1], GROUP):
            out.append(np.concatenate([piece for c in range(a, a + GROUP, P) for piece in
                                       (kblocks(wg[:, c:c + P]).reshape(P, -1), kblocks(wu[:, c:c + P]).reshape(P, -1),
                                        wd[c:c + P])], 1))
        return out

    q = 512
    win, wout = g["hy_w_in"][0], g["hy_w_out"][0]
    heads = [j + 4 * half for j in range(4) for half in range(2)]
    qcols = np.concatenate([np.arange(64 * h, 64 * h + 64) for h in heads])
    wq, wkv, wz, wxbc, wdt = win[:, qcols], win[:, q:q + 256], win[:, 768:1280], win[:, 1280:2048], win[:, 2048:]
    wo = np.concatenate([wout[qcols], wout[q:]], 0)
    hy = tiles(pad(np.concatenate([wq, wkv, wxbc, wz], 1)))
    scw = g["sc_w_in"][0].reshape(D, 3, KB, P)
    sc = tiles(scw.transpose(0, 2, 1, 3).reshape(D, 3 * D)) + tiles(pad(g["sc_w_out"][0]))
    w2 = g["w_in_2"][0]
    W = 512
    part = {n: w2[:, W * i:W * i + W] for i, n in enumerate(("q", "i", "g", "ff", "fb", "dq", "dk", "dv", "dz"))}
    in2 = tiles(np.concatenate([part[n] for n in ("i", "ff", "fb", "q", "g", "dz", "dq", "dk", "dv")], 1))
    parts = {
        "ada0": ada(g["ada_w"][0]), "hy": hy, "hyo": tiles(pad(wo)),
        "ffn0": ffn(g["ffn_w_gate"][0], g["ffn_w_up"][0], g["ffn_w_down"][0]),
        "ada1": ada(g["ada_w"][1]), "sc": sc,
        "ffn1": ffn(g["ffn_w_gate"][1], g["ffn_w_up"][1], g["ffn_w_down"][1]),
        "mod2": ada(g["w_mod_2"][0]), "in2": in2, "out2": tiles(pad(g["w_out_2"][0])),
        "moe": [t for e in range(EXPERTS) for t in ffn(g["w_gate_2"][0, e], g["w_up_2"][0, e], g["w_down_2"][0, e])],
    }
    stream = np.stack([t for n, _ in STREAM for t in parts[n]])
    assert stream.shape == (NTILES, P, TILE)

    i = np.arange(P)
    u, t_ = i[:, None], i[None, :]
    col = lambda a: np.ascontiguousarray(a.reshape(-1, P).T)
    row = lambda a: np.broadcast_to(a.reshape(1, -1), (P, a.size))

    def span(d):
        out = []
        for h in LEVELS:
            mid = t_ // (2 * h) * (2 * h) + h
            right, left = t_ >= mid, t_ < mid
            if d == 0:
                out.append((right & (u >= mid) & (u <= t_)) | (left & (u > t_) & (u < mid)))
            else:
                out.append((left & (u >= t_) & (u < mid)) | (right & (u >= mid) & (u < t_)))
        out.append(u <= t_ if d == 0 else u >= t_)
        return np.concatenate(out, 1)

    def level_masks():
        return [(u // (2 * h) == t_ // (2 * h)) & (u % (2 * h) < h) & (t_ % (2 * h) >= h) for h in LEVELS]

    masks = level_masks()
    rot = np.zeros((P, P), f)
    rot[i[0::2], i[1::2]] = 1
    rot[i[1::2], i[0::2]] = -1
    tok = np.arange(T)
    inv = (1.0 / (f(10000.0) ** (np.arange(0, 32, 2, dtype=f) / f(32)))).astype(f)
    ang = np.concatenate([(tok // 64).astype(f)[:, None] * inv, (tok % 64).astype(f)[:, None] * inv], 1).T
    ang = ang[(i % 64) // 2]
    cols = {
        "ident": np.eye(P), "triF": u <= t_, "triB": u >= t_, "afterF": u > t_, "afterB": u < t_,
        "ones": np.ones((P, P)), "pair": u // 64 == t_ // 64, "rot": rot, "cos": np.cos(ang), "sin": np.sin(ang),
        "spanF": span(0), "spanB": span(1), "maskF": np.concatenate(masks, 1),
        "maskB": np.concatenate([m.T for m in masks], 1),
        "c": np.stack([col(g["c"][0]), col(g["c_ctx"])], 2).reshape(P, -1),
        "c2": np.stack([col(g["c_2"][0]), col(g["c_ctx_2"])], 2).reshape(P, -1),
        "ada_b0": col(g["ada_b"][0]), "ada_b1": col(g["ada_b"][1]), "mod_b2": col(g["b_mod_2"][0]),
        "norm_mix0": col(g["norm_mix"][0]), "norm_mix1": col(g["norm_mix"][1]),
        "norm_ffn0": col(g["norm_ffn"][0]), "norm_ffn1": col(g["norm_ffn"][1]), "final1": col(g["final_norm"]),
        "norm1_2": col(g["norm1_w_2"][0]), "norm2_2": col(g["norm2_w_2"][0]), "final2": col(g["final_norm_w_2"]),
        "qn": np.tile(g["hy_q_norm"][0], 2)[:, None], "kn": np.tile(g["hy_k_norm"][0], 2)[:, None],
        "eps": np.full((P, 1), EPS),
        "conv_w": g["hy_conv_w"][0].reshape(3, 6, P).transpose(2, 1, 0).reshape(P, -1),
        "conv_b": col(g["hy_conv_b"][0]), "dt_bias": row(g["hy_dt_bias"][0]), "a_log": row(g["hy_a_log"][0]),
        "d_skip": col(np.repeat(g["hy_d_skip"][0], 64)), "ssm_norm": col(g["hy_ssm_norm"][0]),
        "w_dt": kblocks(wdt).reshape(P, -1),
        "sc_conv": g["sc_conv_w"][0].reshape(3, KB, P).transpose(2, 1, 0).reshape(P, -1),
        "hg_norm": g["hg_norm_w_2"][0][:, None], "dn_norm": g["dn_norm_w_2"][0][:, None],
        "dn_conv": g["dn_conv_w_2"][0].reshape(9, 12, P).transpose(2, 1, 0).reshape(P, -1),
        "dn_alog": row(g["dn_a_log_2"][0]), "dn_dtb": row(g["dn_dt_bias_2"][0]),
        "w_ba": kblocks(w2[:, 9 * W:]).reshape(P, -1),
        "w_rt": kblocks(np.concatenate([g["w_group_2"][0], g["w_expert_2"][0]], 1)).reshape(P, -1),
        "b_rt": row(np.concatenate([g["b_group_2"][0], g["b_expert_2"][0]])),
        "first4": row(np.array([4, 3, 2, 1])),
    }
    params = np.concatenate([np.asarray(cols[n], f).reshape(P, w) for n, w in COLS], 1)

    def tokens(a):
        return np.ascontiguousarray(a[0].T.reshape(KB, P, T).transpose(1, 0, 2))

    return {"stream": stream, "params": params, "xin": tokens(g["x"]), "ctx1": tokens(g["ctx"]),
            "ctx2": tokens(g["ctx_2"])}


def kernel(**inputs):
    import concourse.bacc as bacc
    from concourse import mybir
    from concourse.bass_utils import run_bass_kernel_spmd
    arrays = _host(inputs)
    nc = bacc.Bacc("TRN2", target_bir_lowering=False, num_devices=1)
    aps = {n: nc.dram_tensor(n, a.shape, mybir.dt.float32, kind="ExternalInput").ap() for n, a in arrays.items()}
    out = nc.dram_tensor("out", (P, KB, T), mybir.dt.float32, kind="ExternalOutput").ap()
    build(nc, out=out, **aps)
    r = run_bass_kernel_spmd(nc, [arrays], core_ids=[0])
    return np.ascontiguousarray(r.results[0]["out"].transpose(1, 0, 2).reshape(D, T).T[None])
```
